# Optimizing a Trainium2 kernel written in Bass

```python
import jax, jax.numpy as jnp
from jax import lax
import numpy as np

D_MODEL = 1024
BATCH = 1
SEQ = 1024
DEPTH = 1

HEAD_DIM = 128
N_Q_HEADS = D_MODEL // HEAD_DIM
N_KV_HEADS = 2
D_ATTN = N_Q_HEADS * HEAD_DIM
D_KV = N_KV_HEADS * HEAD_DIM
WINDOW = 128
BLOCK = 128
ROPE_THETA = 10000.0
D_RNN = (5 * D_MODEL) // 4
RNN_BLOCK_W = 128
N_RNN_BLOCKS = D_RNN // RNN_BLOCK_W
CONV_W = 4
CONV_LEFT = 2
LRU_C = 8.0
N_DIRS = 2
ALPHA = (2.0 * DEPTH) ** 0.25
BETA = (8.0 * DEPTH) ** -0.25
LN_EPS = 1e-5

kernel_name = "hybrid_swa_rglru_deepnorm_encoder"

def _rope(t, pos):
    half = HEAD_DIM // 2
    inv = ROPE_THETA ** (-jnp.arange(half, dtype=jnp.float32) * (2.0 / HEAD_DIM))
    ang = pos.astype(jnp.float32)[:, None] * inv[None, :]
    cos = jnp.cos(ang)[None, :, None, :]
    sin = jnp.sin(ang)[None, :, None, :]
    t32 = t.astype(jnp.float32)
    t1, t2 = t32[..., :half], t32[..., half:]
    out = jnp.concatenate([t1 * cos - t2 * sin, t2 * cos + t1 * sin], axis=-1)
    return out.astype(t.dtype)

def _window_attention(q, k, v, sink):
    B, S = q.shape[0], q.shape[1]
    nb = S // BLOCK
    G = N_Q_HEADS // N_KV_HEADS
    qb = q.astype(jnp.float32).reshape(B, nb, BLOCK, N_KV_HEADS, G, HEAD_DIM)

    def band(t):
        tp = jnp.pad(t.astype(jnp.float32).reshape(B, nb, BLOCK, N_KV_HEADS, HEAD_DIM),
                     ((0, 0), (1, 1), (0, 0), (0, 0), (0, 0)))
        return jnp.concatenate([tp[:, :-2], tp[:, 1:-1], tp[:, 2:]], axis=2)

    kb, vb = band(k), band(v)
    s = jnp.einsum('bnqhgd,bnkhd->bnhgqk', qb, kb) * (HEAD_DIM ** -0.5)
    blk = jnp.arange(nb)[:, None]
    qpos = blk * BLOCK + jnp.arange(BLOCK)[None, :]
    kpos = (blk - 1) * BLOCK + jnp.arange(3 * BLOCK)[None, :]
    valid = ((jnp.abs(qpos[:, :, None] - kpos[:, None, :]) <= WINDOW)
             & (kpos[:, None, :] >= 0) & (kpos[:, None, :] < S))
    s = jnp.where(valid[None, :, None, None], s, -jnp.inf)
    sk = sink.astype(jnp.float32).reshape(N_KV_HEADS, G)[None, None, :, :, None, None]
    m = jnp.maximum(jnp.max(s, axis=-1, keepdims=True), sk)
    p = jnp.exp(s - m)
    denom = jnp.sum(p, axis=-1, keepdims=True) + jnp.exp(sk - m)
    o = jnp.einsum('bnhgqk,bnkhd->bnqhgd', p / denom, vb)
    return o.reshape(B, S, N_Q_HEADS * HEAD_DIM).astype(q.dtype)

def _centred_depthwise_conv(u, w, b):
    S = u.shape[1]
    up = jnp.pad(u, ((0, 0), (CONV_LEFT, CONV_W - 1 - CONV_LEFT), (0, 0)))
    y = b
    for j in range(CONV_W):
        y = y + w[j] * up[:, j:j + S]
    return y

def _linear_scan(a, u, reverse):
    def step(h, au):
        a_t, u_t = au
        h = a_t * h + u_t
        return h, h
    h0 = jnp.zeros((a.shape[0], a.shape[2]), jnp.float32)
    _, hs = lax.scan(step, h0, (jnp.swapaxes(a, 0, 1), jnp.swapaxes(u, 0, 1)), reverse=reverse)
    return jnp.swapaxes(hs, 0, 1)

def _bidirectional_rglru(xc, wa, ba, wx, bx, lam):
    B, S = xc.shape[0], xc.shape[1]
    x32 = xc.astype(jnp.float32)
    xb = x32.reshape(B, S, N_RNN_BLOCKS, RNN_BLOCK_W)
    r = jax.nn.sigmoid(jnp.einsum('bsni,dnij->bsdnj', xb, wa.astype(jnp.float32))
                       .reshape(B, S, N_DIRS, D_RNN) + ba.astype(jnp.float32))
    i = jax.nn.sigmoid(jnp.einsum('bsni,dnij->bsdnj', xb, wx.astype(jnp.float32))
                       .reshape(B, S, N_DIRS, D_RNN) + bx.astype(jnp.float32))
    log_a = -LRU_C * r * jax.nn.softplus(-lam.astype(jnp.float32))
    a = jnp.exp(log_a)
    u = jnp.sqrt(-jnp.expm1(2.0 * log_a)) * (i * x32[:, :, None, :])
    h_fwd = _linear_scan(a[:, :, 0], u[:, :, 0], reverse=False)
    h_bwd = _linear_scan(a[:, :, 1], u[:, :, 1], reverse=True)
    return (h_fwd + h_bwd).astype(xc.dtype)

def _layernorm(x, g, b):
    x32 = x.astype(jnp.float32)
    mu = jnp.mean(x32, axis=-1, keepdims=True)
    var = jnp.mean(jnp.square(x32 - mu), axis=-1, keepdims=True)
    y = (x32 - mu) * lax.rsqrt(var + LN_EPS) * g.astype(jnp.float32) + b.astype(jnp.float32)
    return y.astype(x.dtype)

def setup_inputs(seed: int = 0) -> dict:
    key = jax.random.key(seed)
    ks = jax.random.split(key, 20)
    total = 2 * D_ATTN + 2 * D_KV + 2 * D_RNN + 2 * D_MODEL
    f32 = jnp.float32
    x = jax.random.normal(ks[0], (BATCH, SEQ, D_MODEL), f32)
    col_scale = jnp.concatenate([
        jnp.ones((D_ATTN + D_KV,), f32),
        jnp.full((D_KV,), BETA, f32),
        jnp.ones((D_ATTN + 2 * D_RNN + 2 * D_MODEL,), f32)])
    w_in = jax.random.normal(ks[1], (DEPTH, D_MODEL, total), f32) * (D_MODEL ** -0.5) * col_scale
    b_in = 0.01 * jax.random.normal(ks[2], (DEPTH, total), f32)
    attn_sink = 0.5 * jax.random.normal(ks[3], (DEPTH, N_Q_HEADS), f32)
    conv_w = 0.5 * jax.random.normal(ks[4], (DEPTH, CONV_W, D_RNN), f32)
    conv_b = 0.01 * jax.random.normal(ks[5], (DEPTH, D_RNN), f32)
    gshape = (DEPTH, N_DIRS, N_RNN_BLOCKS, RNN_BLOCK_W, RNN_BLOCK_W)
    lru_wa = jax.random.normal(ks[6], gshape, f32) * (RNN_BLOCK_W ** -0.5)
    lru_ba = 0.01 * jax.random.normal(ks[7], (DEPTH, N_DIRS, D_RNN), f32)
    lru_wx = jax.random.normal(ks[8], gshape, f32) * (RNN_BLOCK_W ** -0.5)
    lru_bx = 0.01 * jax.random.normal(ks[9], (DEPTH, N_DIRS, D_RNN), f32)
    a_c = jax.random.uniform(ks[10], (DEPTH, N_DIRS, D_RNN), f32, 0.9, 0.999)
    a0 = a_c ** (1.0 / LRU_C)
    lru_lambda = jnp.log(a0) - jnp.log1p(-a0)
    w_branch_attn = jax.random.normal(ks[11], (DEPTH, D_ATTN, D_MODEL), f32) * (D_ATTN ** -0.5) * BETA
    w_branch_rnn = jax.random.normal(ks[12], (DEPTH, D_RNN, D_MODEL), f32) * (D_RNN ** -0.5) * BETA
    w_out = jax.random.normal(ks[13], (DEPTH, D_MODEL, D_MODEL), f32) * (D_MODEL ** -0.5) * BETA
    b_out = 0.01 * jax.random.normal(ks[14], (DEPTH, D_MODEL), f32)
    ln_gain = 1.0 + 0.02 * jax.random.normal(ks[15], (DEPTH, D_MODEL), f32)
    ln_bias = 0.02 * jax.random.normal(ks[16], (DEPTH, D_MODEL), f32)
    return {"x": x, "w_in": w_in, "b_in": b_in, "attn_sink": attn_sink,
            "conv_w": conv_w, "conv_b": conv_b, "lru_wa": lru_wa, "lru_ba": lru_ba,
            "lru_wx": lru_wx, "lru_bx": lru_bx, "lru_lambda": lru_lambda,
            "w_branch_attn": w_branch_attn, "w_branch_rnn": w_branch_rnn,
            "w_out": w_out, "b_out": b_out, "ln_gain": ln_gain, "ln_bias": ln_bias}

def reference(x, w_in, b_in, attn_sink, conv_w, conv_b, lru_wa, lru_ba, lru_wx, lru_bx,
              lru_lambda, w_branch_attn, w_branch_rnn, w_out, b_out, ln_gain, ln_bias):
    B, S = x.shape[0], x.shape[1]
    sizes = (D_ATTN, D_KV, D_KV, D_ATTN, D_RNN, D_RNN, D_MODEL, D_MODEL)
    split_at = [int(c) for c in np.cumsum(sizes)[:-1]]
    pos = jnp.arange(S)
    for l in range(DEPTH):
        proj = jnp.einsum('bsd,de->bse', x, w_in[l]) + b_in[l]
        q, k, v, g_attn, x_rnn, g_rnn, m_attn, m_rnn = jnp.split(proj, split_at, axis=-1)
        q = _rope(q.reshape(B, S, N_Q_HEADS, HEAD_DIM), pos)
        k = _rope(k.reshape(B, S, N_KV_HEADS, HEAD_DIM), pos)
        v = v.reshape(B, S, N_KV_HEADS, HEAD_DIM)
        attn = _window_attention(q, k, v, attn_sink[l]) * jax.nn.silu(g_attn)
        xc = _centred_depthwise_conv(x_rnn, conv_w[l], conv_b[l])
        rnn = _bidirectional_rglru(xc, lru_wa[l], lru_ba[l], lru_wx[l], lru_bx[l],
                                   lru_lambda[l]) * jax.nn.silu(g_rnn)
        merged = (jax.nn.sigmoid(m_attn) * jnp.einsum('bse,ed->bsd', attn, w_branch_attn[l])
                  + jax.nn.sigmoid(m_rnn) * jnp.einsum('bse,ed->bsd', rnn, w_branch_rnn[l]))
        out = jnp.einsum('bsd,de->bse', merged, w_out[l]) + b_out[l]
        x = _layernorm(ALPHA * x + out, ln_gain[l], ln_bias[l])
    return x


_drawn_inputs = setup_inputs


def setup_inputs(seed=0):
    import zlib

    import numpy as np

    out = dict(_drawn_inputs(seed))
    spreads = {}
    factors = {'b_in': 6.366,
     'attn_sink': 22.57,
     'conv_b': 5.991,
     'lru_ba': 200.0,
     'lru_bx': 64.0,
     'w_branch_attn': 8.0,
     'b_out': 6.85,
     'ln_gain': 23.453,
     'ln_bias': 23.418}
    for name, (base, spread) in spreads.items():
        noise = np.random.default_rng([zlib.crc32(name.encode()), seed]).standard_normal(out[name].shape)
        drawn = base * np.exp(spread * noise) if base else spread * noise
        out[name] = __import__('jax').numpy.asarray(drawn.astype(out[name].dtype))
    for name, factor in factors.items():
        out[name] = (out[name] * factor).astype(out[name].dtype)
    return out
```

```python
import numpy as np
import concourse.bass as bass
from concourse import mybir
from contextlib import ExitStack

P = 128
D_MODEL, SEQ = 1024, 1024
HEAD_DIM, N_HEADS, N_GROUPS = 128, 8, 2
HEADS = N_HEADS // N_GROUPS
D_RNN = 1280
RNN_BLOCKS = D_RNN // P
PAIRS = RNN_BLOCKS // 2
KT = D_MODEL // P
NB = SEQ // P
HALF = 512
UNIT = KT * P
CONV_W, CONV_LEFT = 4, 2
SCALE = HEAD_DIM ** -0.5
ALPHA = 2.0 ** 0.25
LN_EPS = 1e-5
LRU_C = 8.0
ROPE_THETA = 10000.0
MASKED = -1.0e30

UNITS_GROUP = 2 + 2 * HEADS + 4
UNITS_A = N_GROUPS * UNITS_GROUP
UNITS_PAIR = 8
UNITS_B = 6 + (PAIRS - 1) * UNITS_PAIR + 2
UNITS_AB = UNITS_A + UNITS_B
COLS_PAIR = 7 * UNIT
COLS_B0 = UNITS_A * UNIT
COLS_B1 = COLS_B0 + 5 * UNIT
COLS_B2 = COLS_B1 + (PAIRS - 1) * COLS_PAIR
COLS_C = COLS_B2 + 2 * UNIT
COLS = COLS_C + (2 * KT + 8) * UNIT

F0_GROUP, F1_GROUP = 1 + HEADS + 4, 2 + HEADS + 4
F0_A, F1_A = N_GROUPS * F0_GROUP, N_GROUPS * F1_GROUP
F_PAIR = 6
F0_AB, F1_AB = F0_A + PAIRS * F_PAIR, F1_A + PAIRS * F_PAIR

B_IN, CONV_WEIGHT, CONV_BIAS, GATE_A, GATE_X, LAMBDA = 0, 56, 96, 106, 126, 146
N_SMALL = 166
B_RNN = N_GROUPS * (2 + 2 * HEADS)
B_MERGE = B_RNN + 2 * RNN_BLOCKS
T_COS, T_SIN, T_MASK, T_IDENT = 0, SEQ, 2 * SEQ, 2 * SEQ + 3 * P
N_TABLE = 2 * SEQ + 4 * P


def encoder_layer(nc, x_t, x_rows, stream, small, tables, sink, b_out, ln_gain, ln_bias, out):
    f32, f32r = mybir.dt.float32, mybir.dt.float32r
    ALU, ACT = mybir.AluOpType, mybir.ActivationFunctionType
    ds = bass.ds
    ctx = ExitStack()
    with ctx:
        def allot(where, name, shape, dt=f32):
            return where.enter_context(nc.sbuf_tensor(name, shape, dt))

        raw = allot(ctx, "raw", [P, 2, UNIT])
        w_hi = allot(ctx, "w_hi", [P, 2, UNIT], f32r)
        w_lo = allot(ctx, "w_lo", [P, 2, UNIT], f32r)
        par = allot(ctx, "par", [P, N_SMALL])
        half_b = allot(ctx, "half_b", [P, B_RNN])
        rate = allot(ctx, "rate", [P, 2 * RNN_BLOCKS])
        nrate = allot(ctx, "nrate", [P, 2 * RNN_BLOCKS])
        nsink = allot(ctx, "nsink", [P, N_HEADS])
        nsink_now = allot(ctx, "nsink_now", [P, 1])
        neg_max = allot(ctx, "neg_max", [P, 1])
        denom = allot(ctx, "denom", [P, 1])
        rdenom = allot(ctx, "rdenom", [P, 1])
        stats = allot(ctx, "stats", [P, NB, 2, 6])
        moments = allot(ctx, "moments", [P, NB, 2])
        norm = allot(ctx, "norm", [P, NB, 4])

        norm_scratch = allot(ctx, "norm_scratch", [P, 3, 2 * RNN_BLOCKS])

        with ExitStack() as later:
            wo1_hi = allot(later, "wo1_hi", [P, KT, HALF], f32r)
            wo1_lo = allot(later, "wo1_lo", [P, KT, HALF], f32r)
            rows = allot(later, "rows", [P, NB, D_MODEL])
        xt_hi = allot(ctx, "xt_hi", [P, KT, SEQ], f32r)
        xt_lo = allot(ctx, "xt_lo", [P, KT, SEQ], f32r)

        with ExitStack() as stage:
            x_raw = None
            with ExitStack() as first:
                x_raw = allot(first, "x_raw", [P, KT, SEQ])
            at_hi = allot(stage, "at_hi", [P, HEADS * SEQ // 2], f32r)
            at_hi2 = allot(stage, "at_hi2", [P, HEADS * SEQ // 2], f32r)
            at_lo = allot(stage, "at_lo", [P, HEADS * SEQ // 2], f32r)
            at_lo2 = allot(stage, "at_lo2", [P, HEADS * SEQ // 2], f32r)
            k_hi = allot(stage, "k_hi", [P, SEQ], f32r)
            k_lo = allot(stage, "k_lo", [P, SEQ], f32r)
            v_hi = allot(stage, "v_hi", [P, SEQ], f32r)
            v_lo = allot(stage, "v_lo", [P, SEQ], f32r)
            q_hi = allot(stage, "q_hi", [P, SEQ], f32r)
            q_lo = allot(stage, "q_lo", [P, SEQ], f32r)
            pt_hi = allot(stage, "pt_hi", [P, 12, P], f32r)
            pt_lo = allot(stage, "pt_lo", [P, 12, P], f32r)
            gate = allot(stage, "gate", [P, SEQ])
            tanh_g = allot(stage, "tanh_g", [P, SEQ])
            rot_a = allot(stage, "rot_a", [P, SEQ])
            rot_b = allot(stage, "rot_b", [P, SEQ])
            gated = allot(stage, "gated", [P, SEQ])
            masked = allot(stage, "masked", [P, 3 * P + 1])
            probs = allot(stage, "probs", [P, 2, 3 * P + 1])
            part = allot(stage, "part", [P, 2, SEQ])
            table = allot(stage, "table", [P, N_TABLE])
        with ExitStack() as stage:
            merged_hi = allot(stage, "merged_hi", [P, KT, SEQ], f32r)
            merged_lo = allot(stage, "merged_lo", [P, KT, SEQ], f32r)
            wo0_hi = allot(stage, "wo0_hi", [P, KT, HALF], f32r)
            wo0_lo = allot(stage, "wo0_lo", [P, KT, HALF], f32r)
            with ExitStack() as last:
                gain = allot(last, "gain", [P, D_MODEL])
                shift = allot(last, "shift", [P, D_MODEL])
                bias_o = allot(last, "bias_o", [P, D_MODEL])
            attn_in = allot(stage, "attn_in", [P, 2, SEQ])
            gate_a = allot(stage, "gate_a", [P, SEQ])
            gate_r = allot(stage, "gate_r", [P, SEQ])
        with ExitStack() as stage:
            racc = allot(stage, "racc", [P, KT, SEQ])
            h_hi = [allot(stage, f"h_hi{i}", [P, 2, SEQ], f32r) for i in range(2)]
            h_lo = [allot(stage, f"h_lo{i}", [P, 2, SEQ], f32r) for i in range(2)]
            padded = allot(stage, "padded", [P, SEQ + CONV_W])
            conv = allot(stage, "conv", [P, SEQ])
            conv_hi = allot(stage, "conv_hi", [P, SEQ], f32r)
            conv_lo = allot(stage, "conv_lo", [P, SEQ], f32r)
            silu_g = allot(stage, "silu_g", [P, SEQ])
            decay = [allot(stage, f"decay{i}", [P, SEQ]) for i in range(2)]
            root = [allot(stage, f"root{i}", [P, SEQ]) for i in range(2)]
            state = [allot(stage, f"state{i}", [P, SEQ]) for i in range(2)]
            square = allot(stage, "square", [P, SEQ])

        buf = [ctx.enter_context(nc.psum_tensor(f"proj{i}", [P, 2 * HALF], f32)) for i in range(2)]
        aux = [ctx.enter_context(nc.psum_tensor(f"aux{i}", [P, 2 * HALF], f32)) for i in range(2)]
        s_ps, pt_ps, ot_ps = aux[0][:, 0:HALF], aux[0][:, HALF:2 * HALF], aux[1]
        spill = nc.dram_tensor("spill", (N_GROUPS, P, KT * SEQ), f32, kind="Internal").ap()

        def sem(name):
            return ctx.enter_context(nc.semaphore(name))

        x_landed = [sem(f"x_landed{k}") for k in range(KT)]
        small_landed = sem("small_landed")
        table_landed = sem("table_landed")
        raw_landed = [sem(f"raw_landed{i}") for i in range(2)]
        unit_split = sem("unit_split")
        unit_begun = sem("unit_begun")
        x_hi_done = sem("x_hi_done")
        x_split = sem("x_split")
        filled = [sem(f"filled{i}") for i in range(2)]
        freed = [sem(f"freed{i}") for i in range(2)]
        consts_act = sem("consts_act")
        dve_chain = sem("dve_chain")
        act_chain = sem("act_chain")
        roped = sem("roped")
        roped_hi = sem("roped_hi")
        roped_split = sem("roped_split")
        v_hi_done = sem("v_hi_done")
        silu_done = sem("silu_done")
        scores_done = sem("scores_done")
        scores_masked = sem("scores_masked")
        exp_done = sem("exp_done")
        probs_ready = sem("probs_ready")
        pt_done = sem("pt_done")
        pt_hi_done = sem("pt_hi_done")
        pt_split = sem("pt_split")
        pv_done = sem("pv_done")
        attn_gated = sem("attn_gated")
        attn_hi_done = sem("attn_hi_done")
        attn_split = sem("attn_split")
        spilled = [sem(f"spilled{i}") for i in range(2)]
        racc_zero = sem("racc_zero")
        conv_begun = sem("conv_begun")
        convolved = sem("convolved")
        conv_hi_done = sem("conv_hi_done")
        conv_split = sem("conv_split")
        conv_used = sem("conv_used")
        sigm_g_done = sem("sigm_g_done")
        gate_filled = [sem(f"gate_filled{i}") for i in range(2)]
        gate_freed = [sem(f"gate_freed{i}") for i in range(2)]
        squared = sem("squared")
        one_less = sem("one_less")
        rooted = sem("rooted")
        rnn_done = sem("rnn_done")
        rnn_hi_done = sem("rnn_hi_done")
        rnn_split = sem("rnn_split")
        attn_in_landed = sem("attn_in_landed")
        attn_in_used = sem("attn_in_used")
        merged_done = sem("merged_done")
        merged_hi_done = sem("merged_hi_done")
        merged_split = sem("merged_split")
        rows_landed = sem("rows_landed")
        ln_landed = sem("ln_landed")
        out_done = sem("out_done")
        out_added = sem("out_added")
        var_done = sem("var_done")
        root_done = sem("root_done")
        scaled_by = sem("scaled_by")
        normed = sem("normed")
        gained = sem("gained")
        shifted = sem("shifted")
        stored = sem("stored")
        pool_waited = sem("pool_waited")
        dve_waited = sem("dve_waited")
        pool_chain = sem("pool_chain")
        act_tanh = sem("act_tanh")
        act_decay = sem("act_decay")
        sink_placed = sem("sink_placed")
        rdenom_done = sem("rdenom_done")
        tap_done = sem("tap_done")
        u_done = sem("u_done")
        scanned = sem("scanned")
        mixed = sem("mixed")
        resid = sem("resid")
        stats_done = sem("stats_done")

        def bias(col):
            return par[:, ds(B_IN + col, 1)]

        def at_part(hi, head):
            t = (at_hi, at_hi2) if hi else (at_lo, at_lo2)
            return t[head // 2][:, (head % 2) * SEQ:(head % 2 + 1) * SEQ]

        def key_blocks(n):
            return list(range(max(n - 1, 0), min(n + 1, NB - 1) + 1))

        def pt_segments(n):
            runs = []
            for i, kb in enumerate(key_blocks(n)):
                slot = 3 * (kb % 4) + n - kb + 1
                if runs and slot == runs[-1][2] + 2 * runs[-1][1]:
                    runs[-1][1] += 1
                else:
                    runs.append([i, 1, slot])
            return runs

        def attention_steps():
            return range(NB + 3)

        block = ctx.enter_context(nc.Block())

        @block.sync
        def _(sp):
            def load(index, slot, col, cols=UNIT):
                sp.wait_ge(unit_split, index + 1)
                sp.dma_start(raw[:, slot, 0:cols], stream[:, ds(col, cols)]).then_inc(raw_landed[slot], 16)

            for k in range(2):
                sp.dma_start(x_raw[:, k, :], x_t[:, k, :]).then_inc(x_landed[k], 16)
            for n in range(2):
                sp.wait_ge(unit_split, n + 1)
                sp.dma_start(raw[:, n, :], stream[:, n * UNIT:(n + 1) * UNIT]).then_inc(raw_landed[n], 16)
            for k in range(2, KT):
                sp.dma_start(x_raw[:, k, :], x_t[:, k, :]).then_inc(x_landed[k], 16)
            for n in range(2, UNITS_GROUP):
                load(n, n % 2, n * UNIT)
            with sp.Fori(1, N_GROUPS) as g:
                for n in range(UNITS_GROUP):
                    load(g * UNITS_GROUP + n, n % 2, (g * UNITS_GROUP + n) * UNIT)
            at = COLS_B0
            for n, cols in enumerate((UNIT, UNIT, HALF) * 2):
                load(UNITS_A + n, n % 2, at, cols)
                at += cols
            with sp.Fori(0, (PAIRS - 1) // 2) as pp:
                for j in range(2):
                    at = COLS_B1 + j * COLS_PAIR
                    for n, cols in enumerate((UNIT, UNIT, HALF, UNIT, UNIT, UNIT, UNIT, HALF)):
                        load(pp * (2 * UNITS_PAIR) + UNITS_A + 6 + j * UNITS_PAIR + n, n % 2,
                             pp * (2 * COLS_PAIR) + at, cols)
                        at += cols
            for n in range(2):
                load(UNITS_AB - 2 + n, n, COLS_B2 + n * UNIT)
            for i in range(2):
                sp.wait_ge(spilled[i], 16 * (1 + 4 * N_GROUPS))

            def merge_loads(first_d, first_unit, col):
                with sp.Fori(0, KT // 2) as d:
                    for n in range(2):
                        load(d * 2 + first_unit + n, n, d * (2 * UNIT) + col + n * UNIT)
                    sp.wait_ge(attn_in_used, d + first_d + 1)
                    sp.dma_start(attn_in[:, :, :], spill[:, :, ds(d * SEQ + first_d * SEQ, SEQ)]
                                 .rearrange("g p s -> p g s")).then_inc(attn_in_landed, 16)

            sp.wait_ge(rnn_split, RNN_BLOCKS + 1)
            merge_loads(0, UNITS_AB, COLS_C)
            for n in range(4):
                load(UNITS_AB + KT + n, n % 2, COLS_C + (KT + n) * UNIT)
            merge_loads(KT // 2, UNITS_AB + KT + 4, COLS_C + (KT + 4) * UNIT)
            for n in range(4):
                load(UNITS_AB + 2 * KT + 4 + n, n % 2, COLS_C + (2 * KT + 4 + n) * UNIT)
            sp.wait_ge(filled[0], F0_AB + KT)
            sp.wait_ge(filled[1], F1_AB + KT)
            for n in range(NB):
                sp.dma_start(rows[:, n, :], x_rows[n * P:(n + 1) * P, :]).then_inc(rows_landed, 16)
            sp.wait_ge(merged_split, KT + 1)
            for dst, src in ((bias_o, b_out), (gain, ln_gain), (shift, ln_bias)):
                sp.dma_start(dst[:, :], src.partition_broadcast(P)).then_inc(ln_landed, 16)
            for n in range(NB):
                sp.wait_ge(shifted, n + 1)
                sp.dma_start(out[n * P:(n + 1) * P, :], rows[:, n, :]).then_inc(stored, 16)
            sp.wait_ge(stored, 16 * NB)

        @block.gpsimd
        def _(pool):
            pool.sem_inc(unit_split, 2)

            def split(index, parity, cols, hi, lo, landed, ring=None):
                pool.wait_ge(raw_landed[parity], landed)
                if ring is not None:
                    pool.wait_ge(unit_begun, ring + 1)
                pool.sem_inc(pool_waited, 1)
                nc.gpsimd.tensor_scalar(hi, raw[:, parity, 0:cols], 1.0, 0.0, ALU.mult, ALU.add)\
                    .then_inc(pool_chain, 1)
                pool.wait_ge(pool_chain, index + 1)
                nc.gpsimd.tensor_tensor(lo, raw[:, parity, 0:cols], hi.bitcast(f32), ALU.subtract)\
                    .then_inc(unit_split, 1)

            def ring(index, parity, cols=UNIT, ring_index=None):
                even = index - parity
                split(index, parity, cols, w_hi[:, parity, 0:cols], w_lo[:, parity, 0:cols],
                      even * 8 + 16, index if ring_index is None else ring_index)

            with pool.Fori(0, N_GROUPS) as g:
                for n in range(UNITS_GROUP):
                    ring(g * UNITS_GROUP + n, n % 2)
            for n, cols in enumerate((UNIT, UNIT, HALF) * 2):
                ring(UNITS_A + n, n % 2, cols)
            with pool.Fori(0, (PAIRS - 1) // 2) as pp:
                for j in range(2):
                    for n, cols in enumerate((UNIT, UNIT, HALF, UNIT, UNIT, UNIT, UNIT, HALF)):
                        ring(pp * (2 * UNITS_PAIR) + UNITS_A + 6 + j * UNITS_PAIR + n, n % 2, cols)
            for n in range(2):
                ring(UNITS_AB - 2 + n, n)
            with pool.Fori(0, KT // 2) as d:
                for n in range(2):
                    ring(d * 2 + UNITS_AB + n, n)
            pool.wait_ge(rnn_split, RNN_BLOCKS + 1)
            pool.wait_ge(filled[0], F0_AB)
            pool.wait_ge(filled[1], F1_AB)
            for n in range(4):
                at = UNITS_AB + KT + n
                split(at, n % 2, UNIT, wo0_hi[:, 2 * n:2 * n + 2, :].rearrange("p k c -> p (k c)"),
                      wo0_lo[:, 2 * n:2 * n + 2, :].rearrange("p k c -> p (k c)"), (at - n % 2) * 8 + 16)
            with pool.Fori(0, KT // 2) as d:
                for n in range(2):
                    ring(d * 2 + UNITS_AB + KT + 4 + n, n, ring_index=d * 2 + UNITS_AB + KT + n)
            pool.wait_ge(filled[0], F0_AB + KT)
            pool.wait_ge(filled[1], F1_AB + KT)
            for n in range(4):
                at = UNITS_AB + 2 * KT + 4 + n
                split(at, n % 2, UNIT, wo1_hi[:, 2 * n:2 * n + 2, :].rearrange("p k c -> p (k c)"),
                      wo1_lo[:, 2 * n:2 * n + 2, :].rearrange("p k c -> p (k c)"), (at - n % 2) * 8 + 16)
            pool.wait_ge(ln_landed, 48)
            for n in range(NB):
                pool.wait_ge(gained, n + 1)
                nc.gpsimd.tensor_tensor(rows[:, n, :], rows[:, n, :], shift[:, :], ALU.add)\
                    .then_inc(shifted, 1)

        @block.tensor
        def _(pe):
            pe.sem_inc(unit_begun, 1)
            pe.sem_inc(scores_done, 1)
            pe.sem_inc(pt_done, 2)
            pe.sem_inc(pv_done, NB)

            def part_slice(slot, col, banks, mov_hi, mov_lo, first, last):
                wh, wl = w_hi[:, slot, col:col + P], w_lo[:, slot, col:col + P]
                begun = None
                for h in range(2):
                    i = nc.tensor.matmul(banks[:, h * HALF:(h + 1) * HALF], wh,
                                         mov_hi[:, h * HALF:(h + 1) * HALF], start=first, stop=False)
                    begun = begun or i
                    nc.tensor.matmul(banks[:, h * HALF:(h + 1) * HALF], wh,
                                     mov_lo[:, h * HALF:(h + 1) * HALF], start=False, stop=False)
                for h in range(2):
                    i = nc.tensor.matmul(banks[:, h * HALF:(h + 1) * HALF], wl,
                                         mov_hi[:, h * HALF:(h + 1) * HALF], start=False, stop=last)
                return begun, i

            def tile_slice(k, unit, slot, fill, b, wait_x=False, split_at=None):
                if k == 0:
                    pe.wait_ge(unit_split, (unit if split_at is None else split_at) + 3)
                    pe.wait_ge(freed[b], fill + 1)
                if wait_x:
                    pe.wait_ge(x_split, k + 1)
                first, last = part_slice(slot, k * P, buf[b], xt_hi[:, k, :], xt_lo[:, k, :],
                                         k == 0, k == KT - 1)
                if k == 0:
                    first.then_inc(unit_begun, 1)
                if k == KT - 1:
                    last.then_inc(filled[b], 1)

            def tile(unit, slot, fill, b, wait_x=False, split_at=None):
                for k in range(KT):
                    tile_slice(k, unit, slot, fill, b, wait_x, split_at)

            def scores(m, n):
                pe.wait_ge(scores_masked, m + n + 1)
                ks = key_blocks(n)
                q = slice(n * P, (n + 1) * P)
                keys = slice(ks[0] * P, (ks[-1] + 1) * P)
                dst = s_ps[:, 0:len(ks) * P]
                nc.tensor.matmul(dst, q_hi[:, q], k_hi[:, keys], start=True, stop=False)
                nc.tensor.matmul(dst, q_hi[:, q], k_lo[:, keys], start=False, stop=False)
                nc.tensor.matmul(dst, q_lo[:, q], k_hi[:, keys], start=False, stop=True)\
                    .then_inc(scores_done, 1)

            def transpose_probs(m, n):
                pe.wait_ge(probs_ready, m + n + 2)
                pe.wait_ge(pt_split, m + n + 1)
                nk = len(key_blocks(n))
                for i in range(nk):
                    at = (3 - nk + i) * P
                    last = nc.tensor.transpose(pt_ps[:, i * P:(i + 1) * P], probs[:, n % 2, at:at + P],
                                               table[:, T_IDENT:T_IDENT + P])
                last.then_inc(pt_done, 1)

            def weigh_values(head2, m, kb):
                pe.wait_ge(pt_split, m + min(kb + 1, NB - 1) + 2)
                if kb == 0:
                    pe.wait_ge(attn_gated, head2 + 1)
                if kb == NB // 2 - 1:
                    pe.wait_ge(attn_gated, head2 + 2)
                lo, hi = max(kb - 1, 0), min(kb + 1, NB - 1)
                half = NB // 2
                runs = [(a, z) for a, z in ((lo, min(hi, half - 1)), (max(lo, half), hi)) if a <= z]
                for v, p in ((v_hi, pt_hi), (v_hi, pt_lo), (v_lo, pt_hi)):
                    for a, z in runs:
                        slot = 3 * (kb % 4) + a - kb + 1
                        opens = v is v_hi and p is pt_hi and ((a == 0 and kb == 0) or (a == half and kb == half - 1))
                        last = nc.tensor.matmul(
                            ot_ps[:, a * P:(z + 1) * P], v[:, kb * P:(kb + 1) * P],
                            p[:, slot:slot + z - a + 1, :].rearrange("p n c -> p (n c)"),
                            start=opens, stop=v is v_lo, skip_group_check=True)
                last.then_inc(pv_done, 1)

            def attention(g, h, filler):
                m = g * (HEADS * NB) + h * NB
                at = 0
                for n in attention_steps():
                    if n == 0:
                        pe.wait_ge(roped_split, g * (HEADS + 1) + h + 3)
                    if n < NB:
                        scores(m, n)
                    share = (2 if n < 2 or n >= NB else 1)
                    for _ in range(share - share // 2):
                        at = filler(at)
                    if 1 <= n <= NB:
                        transpose_probs(m, n - 1)
                    for _ in range(share // 2):
                        at = filler(at)
                    if n >= 3:
                        weigh_values(g * (2 * HEADS) + h * 2, m, n - 3)

            def no_filler(at):
                return at

            with pe.Fori(0, N_GROUPS) as g:
                unit = g * UNITS_GROUP
                f0, f1 = g * F0_GROUP, g * F1_GROUP
                tile(unit, 0, f0, 0, wait_x=True)
                tile(unit + 1, 1, f1, 1)
                tile(unit + 2, 0, f0 + 1, 0)
                pe.wait_ge(freed[1], f1 + 2)
                pe.wait_ge(table_landed, 16)
                for n in range(NB):
                    last = nc.tensor.transpose(buf[1][:, n * P:(n + 1) * P], tanh_g[:, n * P:(n + 1) * P],
                                               table[:, T_IDENT:T_IDENT + P])
                last.then_inc(filled[1], 1)
                tile(unit + 3, 1, f1 + 2, 1)

                with pe.Fori(0, HEADS - 1) as h:
                    def next_head(at):
                        b, k = divmod(at, KT)
                        tile_slice(k, unit + h * 2 + 4 + b, b, (f0 + h + 2, f1 + h + 3)[b], b)
                        return at + 1
                    attention(g, h, next_head)
                attention(g, HEADS - 1, no_filler)

                pe.wait_ge(attn_split, g * (2 * HEADS) + 2 * HEADS + 2)
                for n in range(KT // 2):
                    for b in range(2):
                        if b == 0:
                            pe.wait_ge(unit_split, unit + 2 + 2 * HEADS + n + 3)
                        pe.wait_ge(freed[b], (f0 + 1 + HEADS + n + 1, f1 + 2 + HEADS + n + 1)[b])
                        for k in range(HEADS):
                            first, last = part_slice(n % 2, (b * HEADS + k) * P, buf[b], at_part(True, k),
                                                     at_part(False, k), k == 0, k == HEADS - 1)
                            if b == 0 and k == 0:
                                first.then_inc(unit_begun, 1)
                        last.then_inc(filled[b], 1)

            def gates(unit, slot, b_index):
                pe.wait_ge(unit_split, unit + 3)
                pe.wait_ge(conv_split, b_index + 1)
                for n in range(4):
                    a = n % 2
                    pe.wait_ge(gate_freed[a], b_index * 2 + n // 2 + 1)
                    first, last = part_slice(slot, n * P, aux[a], conv_hi, conv_lo, True, True)
                    if n == 0:
                        first.then_inc(unit_begun, 1)
                    last.then_inc(gate_filled[a], 1)

            def rnn_branch(unit, slot, fill0, fill1, blocks_done, h_slot):
                pe.wait_ge(rnn_split, blocks_done + 1)
                for n in range(2):
                    pe.wait_ge(unit_split, unit + n + 3)
                    for j in range(4):
                        b = j % 2
                        pe.wait_ge(freed[b], (fill0, fill1)[b] + 2 * n + j // 2 + 1)
                        for k in range(2):
                            first, last = part_slice((slot + n) % 2, (2 * j + k) * P, buf[b],
                                                     h_hi[h_slot][:, k, :], h_lo[h_slot][:, k, :],
                                                     k == 0, k == 1)
                            if j == 0 and k == 0:
                                first.then_inc(unit_begun, 1)
                        last.then_inc(filled[b], 1)

            pe.wait_ge(scores_masked, N_HEADS * NB + 1)
            pe.wait_ge(pt_split, N_HEADS * NB + 1)
            pe.wait_ge(attn_gated, 2 * N_HEADS + 2)
            for j in range(2):
                u = UNITS_A + 3 * j
                tile(u, j, F0_A + j, 0)
                tile(u + 1, 1 - j, F1_A + j, 1)
                gates(u + 2, j, j)
            with pe.Fori(0, (PAIRS - 1) // 2) as pp:
                for j in range(2):
                    u = pp * (2 * UNITS_PAIR) + UNITS_A + 6 + j * UNITS_PAIR
                    f0 = pp * (2 * F_PAIR) + F0_A + 2 + j * F_PAIR
                    f1 = pp * (2 * F_PAIR) + F1_A + 2 + j * F_PAIR
                    b_index = pp * 4 + 2 + 2 * j
                    tile(u, 0, f0, 0)
                    tile(u + 1, 1, f1, 1)
                    gates(u + 2, 0, b_index)
                    rnn_branch(u + 3, 1, f0 + 1, f1 + 1, b_index, j)
                    tile(u + 5, 1, f0 + 5, 0)
                    tile(u + 6, 0, f1 + 5, 1)
                    gates(u + 7, 1, b_index + 1)
            rnn_branch(UNITS_AB - 2, 0, F0_AB - 4, F1_AB - 4, RNN_BLOCKS, (PAIRS - 1) % 2)

            for first_d, split_at in ((0, UNITS_AB), (KT // 2, UNITS_AB + KT + 4)):
                with pe.Fori(0, KT // 2) as d:
                    tile(None, 0, d + F0_AB + first_d, 0, split_at=d * 2 + split_at)
                    tile(None, 1, d + F1_AB + first_d, 1, split_at=d * 2 + split_at + 1)

            banks = [t[:, h * HALF:(h + 1) * HALF] for t in buf + aux for h in range(2)]
            pe.wait_ge(freed[0], F0_AB + KT + 1)
            pe.wait_ge(freed[1], F1_AB + KT + 1)
            pe.wait_ge(gate_freed[0], 2 * RNN_BLOCKS + 1)
            pe.wait_ge(gate_freed[1], 2 * RNN_BLOCKS + 1)
            pe.wait_ge(merged_split, KT + 1)
            for half, (wh, wl, units) in enumerate(((wo0_hi, wo0_lo, UNITS_AB + KT + 4),
                                                    (wo1_hi, wo1_lo, UNITS_AB + 2 * KT + 8))):
                pe.wait_ge(unit_split, units + 2)
                for n in range(NB):
                    if half:
                        pe.wait_ge(out_added, n + 1)
                    for k in range(KT):
                        s = slice(n * P, (n + 1) * P)
                        nc.tensor.matmul(banks[n], merged_hi[:, k, s], wh[:, k, :], start=k == 0, stop=False)
                        nc.tensor.matmul(banks[n], merged_hi[:, k, s], wl[:, k, :], start=False, stop=False)
                        last = nc.tensor.matmul(banks[n], merged_lo[:, k, s], wh[:, k, :],
                                                start=False, stop=k == KT - 1)
                    last.then_inc(out_done, 1)

        @block.scalar
        def _(act):
            for s, credit in ((exp_done, 1), (gate_freed[0], 1), (gate_freed[1], 1),
                              (spilled[0], 16), (spilled[1], 16), (freed[1], 1)):
                act.sem_inc(s, credit)
            act.dma_start(par[:, :], small).then_inc(small_landed, 16)
            act.dma_start(nsink[:, :], sink.partition_broadcast(P)).then_inc(small_landed, 16)
            act.dma_start(table[:, :], tables).then_inc(table_landed, 16)

            def copy(dst, src):
                return nc.scalar.activation(dst, src, ACT.Copy)

            act.wait_ge(small_landed, 32)
            nc.scalar.activation(half_b[:, :], par[:, B_IN:B_IN + B_RNN], ACT.Copy, scale=0.5)\
                .then_inc(act_chain, 1)
            nc.scalar.activation(nrate[:, :], par[:, LAMBDA:LAMBDA + 2 * RNN_BLOCKS], ACT.Abs)\
                .then_inc(act_chain, 1)
            act.wait_ge(act_chain, 2)
            nc.scalar.activation(nrate[:, :], nrate[:, :], ACT.Exp, scale=-1.0).then_inc(consts_act, 1)
            for k in range(KT):
                act.wait_ge(x_landed[k], 16)
                copy(xt_hi[:, k, :], x_raw[:, k, :]).then_inc(x_hi_done, 1)

            def gate_evac(g, h, fill1, col):
                act.wait_ge(filled[1], fill1 + 1)
                act.wait_ge(attn_gated, g * (2 * HEADS) + h * 2 + 2)
                act.wait_ge(silu_done, g * HEADS + h + 1)
                nc.scalar.activation(gate[:, :], buf[1][:, :], ACT.Identity, scale=0.5,
                                     bias=half_b[:, ds(col, 1)])
                nc.scalar.activation(tanh_g[:, :], buf[1][:, :], ACT.Tanh, scale=0.5,
                                     bias=half_b[:, ds(col, 1)]).then_inc(freed[1], 1)

            def rope_hi(dst, count, last_scores):
                act.wait_ge(roped, count)
                act.wait_ge(scores_done, last_scores + 1)
                copy(dst[:, :], rot_a[:, :]).then_inc(roped_hi, 1)

            def attention(g, h, head, nxt):
                m = g * (HEADS * NB) + h * NB
                for n in attention_steps():
                    if n < NB:
                        nk = len(key_blocks(n))
                        c0 = (3 - nk) * P
                        act.wait_ge(pt_done, m + n + 1)
                        act.wait_ge(scores_masked, m + n + 2)
                        nc.scalar.activation(probs[:, n % 2, c0:3 * P + 1], masked[:, c0:3 * P + 1],
                                             ACT.Exp, scale=-1.0, bias=neg_max[:, 0:1],
                                             accum_out=denom[:, 0:1]).then_inc(exp_done, 1)
                    if 1 <= n <= NB:
                        q = n - 1
                        act.wait_ge(pv_done, m + min(q, NB - 2) + 6)
                        act.wait_ge(pt_done, m + q + 3)
                        runs = pt_segments(q)
                        for i, count, slot in runs:
                            last = copy(pt_hi[:, slot:slot + 2 * count - 1:2, :],
                                        pt_ps[:, i * P:(i + count) * P].rearrange("p (n c) -> p n c", c=P))
                        last.then_inc(pt_hi_done, 1)
                    if n == NB and nxt:
                        rope_hi(q_hi, g * (HEADS + 1) + h + 3, m + NB)
                    if n == NB + 1:
                        attention_hi(g, h, head, 0)
                if nxt:
                    gate_evac(g, h + 1, g * F1_GROUP + h + 3, g * (2 + 2 * HEADS) + h * 2 + 5)
                attention_hi(g, h, head, 1)

            def attention_hi(g, h, head, half):
                act.wait_ge(attn_gated, g * (2 * HEADS) + h * 2 + half + 3)
                copy(head(True)[:, half * HALF:(half + 1) * HALF], gated[:, half * HALF:(half + 1) * HALF])\
                    .then_inc(attn_hi_done, 1)

            with act.Fori(0, N_GROUPS) as g:
                rope_hi(k_hi, g * (HEADS + 1) + 1, g * (HEADS * NB))
                act.wait_ge(filled[1], g * F1_GROUP + 1)
                act.wait_ge(silu_done, g * HEADS + 1)
                nc.scalar.activation(tanh_g[:, :], buf[1][:, :], ACT.Identity,
                                     bias=bias(g * (2 + 2 * HEADS) + 1)).then_inc(freed[1], 1)
                act.wait_ge(filled[1], g * F1_GROUP + 2)
                act.wait_ge(pv_done, g * (HEADS * NB) + NB)
                copy(v_hi[:, :], buf[1][:, :]).then_inc(v_hi_done, 1)
                rope_hi(q_hi, g * (HEADS + 1) + 2, g * (HEADS * NB))
                gate_evac(g, 0, g * F1_GROUP + 2, g * (2 + 2 * HEADS) + 3)
                for h in range(HEADS):
                    attention(g, h, lambda hi, h=h: at_part(hi, h), h < HEADS - 1)
                for n in range(KT // 2):
                    for b in range(2):
                        f = (g * F0_GROUP + 1 + HEADS, g * F1_GROUP + 2 + HEADS)[b] + n
                        act.wait_ge(spilled[b], g * (16 * KT // 2) + 16 * (n + 1))
                        act.wait_ge(filled[b], f + 1)
                        copy(part[:, b, :], buf[b][:, :]).then_inc(freed[b], 1)
                        act.wait_ge(freed[b], f + 2)
                        act.dma_start(spill[ds(g, 1), :, (2 * n + b) * SEQ:(2 * n + b + 1) * SEQ]
                                      .rearrange("g p s -> (g p) s"), part[:, b, :])\
                            .then_inc(spilled[b], 16)

            def rnn_block(b, fill0, fill1, h_slot, j):
                act.wait_ge(convolved, b + 1)
                act.wait_ge(filled[0], fill0 + 1)
                nc.scalar.activation(padded[:, CONV_LEFT:CONV_LEFT + SEQ], buf[0][:, :], ACT.Identity,
                                     bias=bias(b * 2 + B_RNN)).then_inc(freed[0], 1)
                act.wait_ge(freed[0], fill0 + 2)
                act.wait_ge(conv_used, b + 1)
                nc.scalar.activation(conv[:, :], padded[:, 0:SEQ], ACT.Identity,
                                     scale=par[:, ds(b + CONV_WEIGHT, 1)],
                                     bias=par[:, ds(b + CONV_BIAS, 1)]).then_inc(conv_begun, 1)
                act.wait_ge(convolved, b + 2)
                copy(conv_hi[:, :], conv[:, :]).then_inc(conv_hi_done, 1)
                act.wait_ge(rnn_split, b + 1)
                act.wait_ge(filled[1], fill1 + 1)
                nc.scalar.activation(silu_g[:, :], buf[1][:, :], ACT.Sigmoid,
                                     bias=bias(b * 2 + B_RNN + 1)).then_inc(sigm_g_done, 1)
                for n, (dst, first) in enumerate(((decay, GATE_A), (state, GATE_X))):
                    for d in range(2):
                        act.wait_ge(gate_filled[d], b * 2 + n + 1)
                        nc.scalar.activation(dst[d][:, :], aux[d][:, :], ACT.Sigmoid,
                                             bias=par[:, ds(b + first + d * RNN_BLOCKS, 1)])\
                            .then_inc(gate_freed[d], 1)
                for d in range(2):
                    act.wait_ge(gate_freed[d], b * 2 + 2)
                    nc.scalar.activation(root[d][:, :], decay[d][:, :], ACT.Tanh,
                                         scale=rate[:, ds(b + d * RNN_BLOCKS, 1)]).then_inc(act_tanh, 1)
                act.wait_ge(act_tanh, b * 2 + 2)
                for d in range(2):
                    nc.scalar.activation(decay[d][:, :], decay[d][:, :], ACT.Exp,
                                         scale=nrate[:, ds(b + d * RNN_BLOCKS, 1)]).then_inc(act_decay, 1)
                for d in range(2):
                    act.wait_ge(act_decay, b * 2 + d + 1)
                    if d == 1:
                        act.wait_ge(one_less, b * 2 + 1)
                    nc.scalar.activation(square[:, :], decay[d][:, :], ACT.Square).then_inc(squared, 1)
                for d in range(2):
                    act.wait_ge(one_less, b * 2 + d + 1)
                    nc.scalar.activation(root[d][:, :], root[d][:, :], ACT.Sqrt).then_inc(rooted, 1)
                act.wait_ge(rnn_done, b + 1)
                copy(h_hi[h_slot][:, j, :], state[0][:, :]).then_inc(rnn_hi_done, 1)

            act.wait_ge(racc_zero, 1)
            for j in range(2):
                rnn_block(j, F0_A + j, F1_A + j, 0, j)
            with act.Fori(0, (PAIRS - 1) // 2) as pp:
                for i in range(2):
                    f0 = pp * (2 * F_PAIR) + F0_A + 2 + i * F_PAIR
                    f1 = pp * (2 * F_PAIR) + F1_A + 2 + i * F_PAIR
                    for j in range(2):
                        rnn_block(pp * 4 + 2 + 2 * i + j, f0 + 5 * j, f1 + 5 * j, 1 - i, j)

            for first_d in (0, KT // 2):
                with act.Fori(0, KT // 2) as dd:
                    d = dd + first_d
                    act.wait_ge(merged_split, d + 1)
                    for b, dst in enumerate((gate_a, gate_r)):
                        act.wait_ge(filled[b], d + (F0_AB, F1_AB)[b] + 1)
                        nc.scalar.activation(dst[:, :], buf[b][:, :], ACT.Sigmoid,
                                             bias=bias(d * 2 + B_MERGE + b)).then_inc(freed[b], 1)
                    act.wait_ge(merged_done, d + 1)
                    copy(merged_hi[:, ds(d, 1), :].rearrange("p k s -> p (k s)"), gate_a[:, :])\
                        .then_inc(merged_hi_done, 1)

            for n in range(NB):
                act.wait_ge(var_done, n + 1)
                nc.scalar.activation(norm[:, n, 1:2], norm[:, n, 0:1], ACT.Sqrt).then_inc(root_done, 1)
                act.wait_ge(scaled_by, n + 1)
                nc.scalar.activation(rows[:, n, :], rows[:, n, :], ACT.Identity, scale=norm[:, n, 2:3],
                                     bias=norm[:, n, 3:4]).then_inc(normed, 1)

        @block.vector
        def _(dve):
            for s, credit in ((freed[0], 1), (roped_split, 1), (probs_ready, 1), (attn_split, 2), (silu_done, 1), (scores_masked, 1), (pt_split, 1),
                              (attn_gated, 2), (convolved, 1), (conv_used, 1), (rnn_split, 1),
                              (attn_in_used, 1), (merged_split, 1)):
                dve.sem_inc(s, credit)

            def tt(dst, a, b, op):
                return nc.vector.tensor_tensor(dst, a, b, op)

            def stt(dst, a, scalar, b, op0, op1):
                return nc.vector.scalar_tensor_tensor(dst, a, scalar, b, op0, op1)

            steps = [0]

            def link(ins):
                steps[0] += 1
                ins.then_inc(dve_chain, 1)
                dve.wait_ge(dve_chain, steps[0])

            for k in range(KT):
                dve.wait_ge(x_hi_done, k + 1)
                tt(xt_lo[:, k, :], x_raw[:, k, :], xt_hi[:, k, :].bitcast(f32), ALU.subtract)\
                    .then_inc(x_split, 1)
            dve.wait_ge(small_landed, 32)
            link(nc.vector.tensor_scalar(nsink[:, :], nsink[:, :], -1.0, None, ALU.mult))
            dve.wait_ge(consts_act, 1)
            e, s, s2 = nrate[:, :], norm_scratch[:, 0, :], norm_scratch[:, 1, :]
            acc = norm_scratch[:, 2, :]
            link(nc.vector.tensor_scalar(s, e, 2.0, None, ALU.add))
            link(nc.vector.reciprocal(s, s))
            link(tt(s, s, e, ALU.mult))
            link(tt(s2, s, s, ALU.mult))
            link(nc.vector.tensor_scalar(acc, s2, 1.0 / 19, None, ALU.mult))
            for odd in range(17, 1, -2):
                link(stt(acc, acc, 1.0 / odd, s2, ALU.add, ALU.mult))
            link(stt(acc, acc, 1.0, s, ALU.add, ALU.mult))
            link(nc.vector.tensor_scalar(s, par[:, LAMBDA:LAMBDA + 2 * RNN_BLOCKS], -1.0, 0.0,
                                         ALU.mult, ALU.max))
            link(stt(s, acc, 2.0, s, ALU.mult, ALU.add))
            link(nc.vector.tensor_scalar(rate[:, :], s, LRU_C, None, ALU.mult))
            link(nc.vector.tensor_scalar(nrate[:, :], s, -LRU_C, None, ALU.mult))
            dve.wait_ge(table_landed, 16)

            cos, sin = table[:, T_COS:T_COS + SEQ], table[:, T_SIN:T_SIN + SEQ]

            def rope(fill0, col, count):
                dve.wait_ge(filled[0], fill0 + 1)
                dve.wait_ge(roped_split, count)
                b = bias(col)
                stt(rot_a[:, :], buf[0][:, :], b, cos, ALU.add, ALU.mult)
                stt(rot_b[0:64, :], buf[0][64:P, :], par[64:P, ds(B_IN + col, 1)], sin[64:P, :],
                    ALU.add, ALU.mult)
                stt(rot_b[64:P, :], buf[0][0:64, :], par[0:64, ds(B_IN + col, 1)], sin[0:64, :],
                    ALU.add, ALU.mult).then_inc(freed[0], 1)
                dve.wait_ge(freed[0], fill0 + 2)
                tt(rot_a[:, :], rot_a[:, :], rot_b[:, :], ALU.add).then_inc(roped, 1)

            def rope_lo(dst, hi, count):
                dve.wait_ge(roped_hi, count)
                tt(dst[:, :], rot_a[:, :], hi[:, :].bitcast(f32), ALU.subtract).then_inc(roped_split, 1)

            def silu(g, h, fill1):
                dve.wait_ge(freed[1], fill1 + 2)
                stt(gate[:, :], tanh_g[:, :], 1.0, gate[:, :], ALU.add, ALU.mult).then_inc(silu_done, 1)

            def gate_half(g, h, half):
                c = slice(half * HALF, (half + 1) * HALF)
                dve.wait_ge(silu_done, g * HEADS + h + 2)
                dve.wait_ge(attn_split, g * (2 * HEADS) + h * 2 + half + 1)
                dve.wait_ge(pv_done, g * (HEADS * NB) + h * NB + NB + (NB // 2 + 1, NB)[half])
                tt(gated[:, c], ot_ps[:, c], gate[:, c], ALU.mult).then_inc(attn_gated, 1)

            def attention_lo(g, h, head, half):
                c = slice(half * HALF, (half + 1) * HALF)
                dve.wait_ge(attn_hi_done, g * (2 * HEADS) + h * 2 + half + 1)
                tt(head(False)[:, c], gated[:, c], head(True)[:, c].bitcast(f32), ALU.subtract)\
                    .then_inc(attn_split, 1)

            def attention(g, h, head, nxt):
                m = g * (HEADS * NB) + h * NB
                dve.wait_ge(exp_done, m + 1)
                nc.vector.tensor_copy(masked[:, 3 * P:3 * P + 1], nsink[:, ds(g * HEADS + h, 1)])\
                    .then_inc(sink_placed, 1)
                nc.vector.tensor_copy(nsink_now[:, :], nsink[:, ds(g * HEADS + h, 1)])\
                    .then_inc(sink_placed, 1)
                dve.wait_ge(sink_placed, g * (2 * HEADS) + h * 2 + 2)
                for n in attention_steps():
                    if n < NB:
                        nk = len(key_blocks(n))
                        c0 = (3 - nk) * P
                        m0 = T_MASK + (0 if n else P)
                        dve.wait_ge(exp_done, m + n + 1)
                        dve.wait_ge(scores_done, m + n + 2)
                        dve.sem_inc(dve_waited, 1)
                        nc.vector.tensor_tensor_reduce(
                            out=masked[:, c0:3 * P], in0=s_ps[:, 0:nk * P], in1=table[:, m0:m0 + nk * P],
                            scale=-SCALE, scalar=nsink_now[:, 0:1], op0=ALU.add, op1=ALU.min,
                            accum_out=neg_max[:, 0:1]).then_inc(scores_masked, 1)
                        dve.wait_ge(exp_done, m + n + 2)
                        dve.wait_ge(probs_ready, m + n + 1)
                        nc.vector.reciprocal(rdenom[:, :], denom[:, :]).then_inc(rdenom_done, 1)
                        dve.wait_ge(rdenom_done, m + n + 1)
                        nc.vector.tensor_scalar(probs[:, n % 2, c0:3 * P], probs[:, n % 2, c0:3 * P],
                                                rdenom[:, 0:1], None, ALU.mult).then_inc(probs_ready, 1)
                    if 1 <= n <= NB:
                        q = n - 1
                        dve.wait_ge(pt_hi_done, m + q + 1)
                        for i, count, slot in pt_segments(q):
                            at = slice(slot, slot + 2 * count - 1, 2)
                            last = tt(pt_lo[:, at, :],
                                      pt_ps[:, i * P:(i + count) * P].rearrange("p (n c) -> p n c", c=P),
                                      pt_hi[:, at, :].bitcast(f32), ALU.subtract)
                        last.then_inc(pt_split, 1)
                    if n == 6 and nxt:
                        rope(g * F0_GROUP + h + 2, g * (2 + 2 * HEADS) + h * 2 + 4, g * (HEADS + 1) + h + 3)
                    if n == NB and nxt:
                        rope_lo(q_lo, q_hi, g * (HEADS + 1) + h + 3)
                    if n == NB + 1:
                        gate_half(g, h, 0)
                        attention_lo(g, h, head, 0)
                gate_half(g, h, 1)
                if nxt:
                    silu(g, h + 1, g * F1_GROUP + h + 3)
                attention_lo(g, h, head, 1)

            with dve.Fori(0, N_GROUPS) as g:
                rope(g * F0_GROUP, g * (2 + 2 * HEADS), g * (HEADS + 1) + 1)
                rope_lo(k_lo, k_hi, g * (HEADS + 1) + 1)
                rope(g * F0_GROUP + 1, g * (2 + 2 * HEADS) + 2, g * (HEADS + 1) + 2)
                dve.wait_ge(v_hi_done, g + 1)
                tt(v_lo[:, :], buf[1][:, :], v_hi[:, :].bitcast(f32), ALU.subtract).then_inc(freed[1], 1)
                rope_lo(q_lo, q_hi, g * (HEADS + 1) + 2)
                silu(g, 0, g * F1_GROUP + 2)
                for h in range(HEADS):
                    attention(g, h, lambda hi, h=h: at_part(hi, h), h < HEADS - 1)

            dve.wait_ge(filled[0], F0_A)
            dve.wait_ge(filled[1], F1_A)
            for i in range(2):
                dve.wait_ge(spilled[i], 16 * (1 + 4 * N_GROUPS))
            link(nc.vector.memset(padded[:, 0:CONV_LEFT], 0.0))
            nc.vector.memset(padded[:, CONV_LEFT + SEQ:CONV_W + SEQ], 0.0).then_inc(racc_zero, 1)
            nc.vector.memset(racc[:, :, :], 0.0).then_inc(racc_zero, 1)
            dve.wait_ge(racc_zero, 2)

            def rnn_block(b, fill1, h_slot, j, add):
                dve.wait_ge(conv_begun, b + 1)
                for tap in range(1, CONV_W):
                    last = stt(conv[:, :], padded[:, tap:tap + SEQ],
                               par[:, ds(b + CONV_WEIGHT + tap * RNN_BLOCKS, 1)], conv[:, :],
                               ALU.mult, ALU.add)
                    if tap < CONV_W - 1:
                        last.then_inc(tap_done, 1)
                        dve.wait_ge(tap_done, b * (CONV_W - 2) + tap)
                last.then_inc(convolved, 1)
                dve.wait_ge(conv_hi_done, b + 1)
                tt(conv_lo[:, :], conv[:, :], conv_hi[:, :].bitcast(f32), ALU.subtract)\
                    .then_inc(conv_split, 1)
                dve.wait_ge(sigm_g_done, b + 1)
                stt(silu_g[:, :], buf[1][:, :], bias(b * 2 + B_RNN + 1), silu_g[:, :], ALU.add, ALU.mult)\
                    .then_inc(freed[1], 1)
                add(0)
                for d in range(2):
                    dve.wait_ge(gate_freed[d], b * 2 + 3)
                    last = tt(state[d][:, :], state[d][:, :], conv[:, :], ALU.mult)
                last.then_inc(conv_used, 1)
                add(1)
                for d in range(2):
                    dve.wait_ge(squared, b * 2 + d + 1)
                    stt(root[d][:, :], square[:, :], 1.0, root[d][:, :], ALU.add, ALU.mult)\
                        .then_inc(one_less, 1)
                    add(2 + d)
                dve.wait_ge(conv_used, b + 2)
                for d in range(2):
                    dve.wait_ge(rooted, b * 2 + d + 1)
                    tt(state[d][:, :], state[d][:, :], root[d][:, :], ALU.mult).then_inc(u_done, 1)
                    add(4 + 2 * d)
                    dve.wait_ge(u_done, b * 2 + d + 1)
                    if d == 0:
                        nc.vector.tensor_tensor_scan(state[0][:, :], decay[0][:, :], state[0][:, :], 0.0,
                                                     ALU.mult, ALU.add)
                    else:
                        last = nc.vector.tensor_tensor_scan(state[1][:, ::-1], decay[1][:, ::-1],
                                                            state[1][:, ::-1], 0.0, ALU.mult, ALU.add)
                        last.then_inc(scanned, 1)
                    add(5 + 2 * d)
                dve.wait_ge(scanned, b * 2 + 1)
                tt(state[0][:, :], state[0][:, :], state[1][:, :], ALU.add).then_inc(scanned, 1)
                dve.wait_ge(scanned, b * 2 + 2)
                tt(state[0][:, :], state[0][:, :], silu_g[:, :], ALU.mult).then_inc(rnn_done, 1)
                dve.wait_ge(rnn_hi_done, b + 1)
                tt(h_lo[h_slot][:, j, :], state[0][:, :], h_hi[h_slot][:, j, :].bitcast(f32), ALU.subtract)\
                    .then_inc(rnn_split, 1)

            def add_branch(d, fill0, fill1):
                b = d % 2
                dve.wait_ge(filled[b], (fill0, fill1)[b] + d // 2 + 1)
                tt(racc[:, d, :], buf[b][:, :], racc[:, d, :], ALU.add).then_inc(freed[b], 1)

            def nothing(d):
                return None

            for j in range(2):
                rnn_block(j, F1_A + j, 0, j, nothing)
            with dve.Fori(0, (PAIRS - 1) // 2) as pp:
                for i in range(2):
                    f0 = pp * (2 * F_PAIR) + F0_A + 2 + i * F_PAIR
                    f1 = pp * (2 * F_PAIR) + F1_A + 2 + i * F_PAIR
                    rnn_block(pp * 4 + 2 + 2 * i, f1, 1 - i, 0, lambda d: add_branch(d, f0 + 1, f1 + 1))
                    rnn_block(pp * 4 + 3 + 2 * i, f1 + 5, 1 - i, 1, nothing)
            for d in range(KT):
                add_branch(d, F0_AB - 4, F1_AB - 4)

            for first_d in (0, KT // 2):
                with dve.Fori(0, KT // 2) as dd:
                    d = dd + first_d
                    dve.wait_ge(attn_in_landed, d * 16 + 16)
                    tt(attn_in[:, 0, :], attn_in[:, 0, :], attn_in[:, 1, :], ALU.add).then_inc(mixed, 1)
                    dve.wait_ge(freed[1], d + F1_AB + 2)
                    tt(gate_r[:, :], gate_r[:, :], racc[:, ds(d, 1), :].rearrange("p k s -> p (k s)"),
                       ALU.mult)
                    dve.wait_ge(mixed, d + 1)
                    tt(gate_a[:, :], gate_a[:, :], attn_in[:, 0, :], ALU.mult).then_inc(attn_in_used, 1)
                    dve.wait_ge(attn_in_used, d + 2)
                    tt(gate_a[:, :], gate_a[:, :], gate_r[:, :], ALU.add).then_inc(merged_done, 1)
                    dve.wait_ge(merged_hi_done, d + 1)
                    tt(merged_lo[:, ds(d, 1), :].rearrange("p k s -> p (k s)"), gate_a[:, :],
                       merged_hi[:, ds(d, 1), :].rearrange("p k s -> p (k s)").bitcast(f32),
                       ALU.subtract).then_inc(merged_split, 1)

            dve.wait_ge(rows_landed, 16 * NB)
            dve.wait_ge(ln_landed, 48)
            for n in range(NB):
                stt(rows[:, n, :], rows[:, n, :], ALPHA, bias_o[:, :], ALU.mult, ALU.add)\
                    .then_inc(resid, 1)
            for half in range(2):
                c = slice(half * HALF, (half + 1) * HALF)
                for n in range(NB):
                    bank = (buf + aux)[n // 2][:, (n % 2) * HALF:(n % 2 + 1) * HALF]
                    dve.wait_ge(resid, n + 1)
                    dve.wait_ge(out_done, half * NB + n + 1)
                    tt(rows[:, n, c], bank, rows[:, n, c], ALU.add).then_inc(out_added, 1)
                    dve.wait_ge(out_added, half * NB + n + 1)
                    nc.vector.bn_stats(stats[:, n, half, :], rows[:, n, c]).then_inc(stats_done, 1)
                    if half:
                        dve.wait_ge(stats_done, NB + n + 1)
                        link(nc.vector.bn_aggr(moments[:, n, :], stats[:, n, :, :].rearrange("p a b -> p (a b)")))
                        nc.vector.tensor_scalar(norm[:, n, 0:1], moments[:, n, 1:2], LN_EPS, None, ALU.add)\
                            .then_inc(var_done, 1)
                        if n:
                            dve.wait_ge(normed, n)
                            tt(rows[:, n - 1, :], rows[:, n - 1, :], gain[:, :], ALU.mult).then_inc(gained, 1)
                        dve.wait_ge(root_done, n + 1)
                        link(nc.vector.reciprocal(norm[:, n, 2:3], norm[:, n, 1:2]))
                        stt(norm[:, n, 3:4], moments[:, n, 0:1], -1.0, norm[:, n, 2:3], ALU.mult, ALU.mult)\
                            .then_inc(scaled_by, 1)
            dve.wait_ge(normed, NB)
            tt(rows[:, NB - 1, :], rows[:, NB - 1, :], gain[:, :], ALU.mult).then_inc(gained, 1)


def _tables():
    half = HEAD_DIM // 2
    inv = (np.float32(ROPE_THETA) ** (-np.arange(half, dtype=np.float32) * np.float32(2.0 / HEAD_DIM)))
    ang = inv.astype(np.float32)[:, None] * np.arange(SEQ, dtype=np.float32)[None, :]
    cos, sin = np.cos(ang).astype(np.float32), np.sin(ang).astype(np.float32)
    q, k = np.arange(P)[:, None], np.arange(3 * P)[None, :] - P
    mask = np.where(np.abs(q - k) <= P, 0.0, MASKED).astype(np.float32)
    return np.concatenate([np.concatenate([cos, cos]), np.concatenate([sin, -sin]), mask,
                           np.eye(P, dtype=np.float32)], axis=1)


def _stream(w_in, lru_wa, lru_wx, w_attn, w_rnn, w_out):
    def cols(w, at, n=P):
        return w[:, at:at + n].reshape(-1, P, n).transpose(1, 0, 2).reshape(P, -1)

    q0, k0, v0, ga0 = 0, 1024, 1280, 1536
    x0, gr0, ma0, mr0 = 2560, 3840, 5120, 6144
    out = []
    for g in range(N_GROUPS):
        out += [cols(w_in, k0 + g * P), cols(w_in, v0 + g * P)]
        for h in range(g * HEADS, (g + 1) * HEADS):
            out += [cols(w_in, q0 + h * P), cols(w_in, ga0 + h * P)]
        mine = w_attn[g * HEADS * P:(g + 1) * HEADS * P]
        out += [cols(mine, d * P) for d in range(KT)]

    def block(b):
        return [cols(w_in, x0 + b * P), cols(w_in, gr0 + b * P),
                lru_wa[0, b], lru_wa[1, b], lru_wx[0, b], lru_wx[1, b]]

    def branch(p):
        mine = w_rnn[2 * p * P:2 * (p + 1) * P]
        return [cols(mine, d * P) for d in range(KT)]

    out += block(0) + block(1)
    for p in range(1, PAIRS):
        out += block(2 * p) + branch(p - 1) + block(2 * p + 1)
    out += branch(PAIRS - 1)
    for part in range(2):
        for d in range(part * KT // 2, (part + 1) * KT // 2):
            out += [cols(w_in, ma0 + d * P), cols(w_in, mr0 + d * P)]
        out += [cols(w_out, part * HALF, HALF)]
    return np.concatenate(out, axis=1)


def _small(b_in, conv_w, conv_b, ba, bx, lam):
    b = b_in.reshape(56, P)
    q0, k0, v0, ga0, x0, gr0, ma0, mr0 = 0, 8, 10, 12, 20, 30, 40, 48
    order = []
    for g in range(N_GROUPS):
        order += [k0 + g, v0 + g]
        for h in range(g * HEADS, (g + 1) * HEADS):
            order += [q0 + h, ga0 + h]
    for n in range(RNN_BLOCKS):
        order += [x0 + n, gr0 + n]
    for d in range(KT):
        order += [ma0 + d, mr0 + d]
    rows = [b[order], conv_w.reshape(-1, P), conv_b.reshape(-1, P), ba.reshape(-1, P),
            bx.reshape(-1, P), lam.reshape(-1, P)]
    return np.ascontiguousarray(np.concatenate(rows, axis=0).T)


def kernel(x, w_in, b_in, attn_sink, conv_w, conv_b, lru_wa, lru_ba, lru_wx, lru_bx, lru_lambda,
           w_branch_attn, w_branch_rnn, w_out, b_out, ln_gain, ln_bias):
    import concourse.bacc as bacc
    from concourse.bass_utils import run_bass_kernel_spmd as run

    arrays = {
        "x_t": np.ascontiguousarray(np.asarray(x)[0].T.reshape(KT, P, SEQ).transpose(1, 0, 2)),
        "x_rows": np.ascontiguousarray(np.asarray(x)[0]),
        "stream": _stream(*(np.asarray(a)[0] for a in (w_in, lru_wa, lru_wx, w_branch_attn,
                                                       w_branch_rnn, w_out))),
        "small": _small(*(np.asarray(a)[0] for a in (b_in, conv_w, conv_b, lru_ba, lru_bx, lru_lambda))),
        "tables": _tables(),
        "sink": np.ascontiguousarray(np.asarray(attn_sink)[0]),
        "b_out": np.ascontiguousarray(np.asarray(b_out)[0]),
        "ln_gain": np.ascontiguousarray(np.asarray(ln_gain)[0]),
        "ln_bias": np.ascontiguousarray(np.asarray(ln_bias)[0]),
    }
    nc = bacc.Bacc("TRN2", target_bir_lowering=False, num_devices=1)
    args = [nc.dram_tensor(name, a.shape, mybir.dt.from_np(a.dtype), kind="ExternalInput").ap()
            for name, a in arrays.items()]
    args.append(nc.dram_tensor("out", (SEQ, D_MODEL), mybir.dt.float32, kind="ExternalOutput").ap())
    encoder_layer(nc, *args)
    r = run(nc, [arrays], core_ids=[0])
    return r.results[0]["out"].reshape(1, SEQ, D_MODEL)
```

```python
import numpy as np
import concourse.bass as bass
from concourse import mybir
from contextlib import ExitStack

P = 128
D_MODEL, SEQ = 1024, 1024
HEAD_DIM, N_HEADS, N_GROUPS = 128, 8, 2
HEADS = N_HEADS // N_GROUPS
D_RNN = 1280
RNN_BLOCKS = D_RNN // P
PAIRS = RNN_BLOCKS // 2
KT = D_MODEL // P
NB = SEQ // P
HALF = 512
UNIT = KT * P
CONV_W, CONV_LEFT = 4, 2
SCALE = HEAD_DIM ** -0.5
ALPHA = 2.0 ** 0.25
LN_EPS = 1e-5
LRU_C = 8.0
ROPE_THETA = 10000.0
MASKED = -1.0e30

UNITS_GROUP = 2 * HEADS + 2 + 4
UNIT_B = 2 + N_GROUPS * UNITS_GROUP
UNITS_PAIR = 8
UNIT_P = UNIT_B + 4
UNIT_C = UNIT_P + (PAIRS - 1) * UNITS_PAIR
TILES_C = ((1, 2, UNIT_C + 4, 0), (3, 2, UNIT_C + 10, 2), (5, 3, UNIT_C + 16, 4))
UNIT_WO0 = (UNIT_C + 8, UNIT_C + 14)
UNIT_WO1 = UNIT_C + 22
COLS_B = UNIT_B * UNIT
COLS_P = COLS_B + 3 * UNIT
COLS_PAIR = 7 * UNIT
COLS_C = COLS_P + (PAIRS - 1) * COLS_PAIR

FILLS_GROUP = HEADS + 1 + 4
FILL_B = 1 + N_GROUPS * FILLS_GROUP
FILL_X0 = FILL_B - 5
FILL_P = FILL_B + 1
FILLS_PAIR = 6
FILL_C = FILL_P + (PAIRS - 1) * FILLS_PAIR
FILL_D = FILL_C + 5 + KT - 1

B_IN, CONV_WEIGHT, CONV_BIAS, GATE_A, GATE_X, LAMBDA = 0, 56, 96, 106, 126, 146
N_SMALL = 166
B_RNN = N_GROUPS * (2 + 2 * HEADS)
B_MERGE = B_RNN + 2 * RNN_BLOCKS
T_COS, T_SIN, T_MASK, T_IDENT = 0, SEQ, 2 * SEQ, 2 * SEQ + 3 * P
N_TABLE = 2 * SEQ + 4 * P


def encoder_layer(nc, x_t, x_rows, stream, small, tables, sink, b_out, ln_gain, ln_bias, out):
    f32, f32r = mybir.dt.float32, mybir.dt.float32r
    ALU, ACT = mybir.AluOpType, mybir.ActivationFunctionType
    ds = bass.ds
    ctx = ExitStack()
    with ctx:
        def allot(where, name, shape, dt=f32):
            return where.enter_context(nc.sbuf_tensor(name, shape, dt))

        raw = allot(ctx, "raw", [P, 2, UNIT])
        w_hi = allot(ctx, "w_hi", [P, 2, UNIT], f32r)
        w_lo = allot(ctx, "w_lo", [P, 2, UNIT], f32r)
        par = allot(ctx, "par", [P, N_SMALL])
        half_b = allot(ctx, "half_b", [P, B_RNN])
        rate = allot(ctx, "rate", [P, 2 * RNN_BLOCKS])
        nrate = allot(ctx, "nrate", [P, 2 * RNN_BLOCKS])
        nsink = allot(ctx, "nsink", [P, N_HEADS])
        nsink_now = allot(ctx, "nsink_now", [P, 1])
        neg_max = allot(ctx, "neg_max", [P, 1])
        denom = allot(ctx, "denom", [P, 1])
        rdenom = allot(ctx, "rdenom", [P, 1])
        stats = allot(ctx, "stats", [P, NB, 2, 6])
        moments = allot(ctx, "moments", [P, NB, 2])
        norm = allot(ctx, "norm", [P, NB, 4])

        norm_scratch = allot(ctx, "norm_scratch", [P, 3, 2 * RNN_BLOCKS])

        with ExitStack() as later:
            wo1_hi = allot(later, "wo1_hi", [P, KT, HALF], f32r)
            wo1_lo = allot(later, "wo1_lo", [P, KT, HALF], f32r)
            rows = allot(later, "rows", [P, NB, D_MODEL])
        xt_hi = allot(ctx, "xt_hi", [P, KT, SEQ], f32r)
        xt_lo = allot(ctx, "xt_lo", [P, KT, SEQ], f32r)

        with ExitStack() as stage:
            x_raw = None
            with ExitStack() as first:
                x_raw = allot(first, "x_raw", [P, KT, SEQ])
            at_hi = allot(stage, "at_hi", [P, HEADS * SEQ], f32r)
            at_lo = allot(stage, "at_lo", [P, HEADS * SEQ], f32r)
            k_hi = allot(stage, "k_hi", [P, SEQ], f32r)
            k_lo = allot(stage, "k_lo", [P, SEQ], f32r)
            v_hi = allot(stage, "v_hi", [P, SEQ], f32r)
            v_lo = allot(stage, "v_lo", [P, SEQ], f32r)
            q_hi = allot(stage, "q_hi", [P, SEQ], f32r)
            q_lo = allot(stage, "q_lo", [P, SEQ], f32r)
            pt_hi = allot(stage, "pt_hi", [P, 12, P], f32r)
            pt_lo = allot(stage, "pt_lo", [P, 12, P], f32r)
            gate = allot(stage, "gate", [P, SEQ])
            tanh_g = allot(stage, "tanh_g", [P, SEQ])
            rot_a = allot(stage, "rot_a", [P, SEQ])
            rot_b = allot(stage, "rot_b", [P, SEQ])
            gated = allot(stage, "gated", [P, SEQ])
            masked = allot(stage, "masked", [P, 3 * P + 1])
            probs = allot(stage, "probs", [P, 2, 3 * P + 1])
            part = allot(stage, "part", [P, 2, SEQ])
            table = allot(stage, "table", [P, N_TABLE])
        with ExitStack() as stage:
            merged_hi = allot(stage, "merged_hi", [P, KT, SEQ], f32r)
            with ExitStack() as last:
                gain = allot(last, "gain", [P, D_MODEL])
                shift = allot(last, "shift", [P, D_MODEL])
                bias_o = allot(last, "bias_o", [P, D_MODEL])
            gate_a = allot(stage, "gate_a", [P, SEQ])
            gate_r = allot(stage, "gate_r", [P, SEQ])
            attn_in = allot(stage, "attn_in", [P, 2, SEQ])
            wo0_hi = allot(stage, "wo0_hi", [P, KT, HALF], f32r)
            wo0_lo = allot(stage, "wo0_lo", [P, KT, HALF], f32r)
            merged_lo = allot(stage, "merged_lo", [P, KT, SEQ], f32r)
        with ExitStack() as stage:
            racc = allot(stage, "racc", [P, KT, SEQ])
            padded = allot(stage, "padded", [P, SEQ + CONV_W])
            conv = allot(stage, "conv", [P, SEQ])
            conv_hi = allot(stage, "conv_hi", [P, SEQ], f32r)
            conv_lo = allot(stage, "conv_lo", [P, SEQ], f32r)
            silu_g = allot(stage, "silu_g", [P, SEQ])
            decay = [allot(stage, f"decay{i}", [P, SEQ]) for i in range(2)]
            root = [allot(stage, f"root{i}", [P, SEQ]) for i in range(2)]
            state = [allot(stage, f"state{i}", [P, SEQ]) for i in range(2)]
            square = allot(stage, "square", [P, SEQ])
            h_hi = [allot(stage, f"h_hi{i}", [P, 2, SEQ], f32r) for i in range(2)]
            h_lo = [allot(stage, f"h_lo{i}", [P, 2, SEQ], f32r) for i in range(2)]

        buf = [ctx.enter_context(nc.psum_tensor(f"proj{i}", [P, 2 * HALF], f32)) for i in range(2)]
        aux = [ctx.enter_context(nc.psum_tensor(f"aux{i}", [P, 2 * HALF], f32)) for i in range(2)]
        s_ps, pt_ps, ot_ps = aux[0][:, 0:HALF], aux[0][:, HALF:2 * HALF], aux[1]
        spill = nc.dram_tensor("spill", (N_GROUPS, P, KT * SEQ), f32, kind="Internal").ap()

        def sem(name):
            return ctx.enter_context(nc.semaphore(name))

        x_landed = [sem(f"x_landed{k}") for k in range(KT)]
        small_landed = sem("small_landed")
        table_landed = sem("table_landed")
        raw_landed = [sem(f"raw_landed{i}") for i in range(2)]
        unit_split = sem("unit_split")
        unit_begun = sem("unit_begun")
        x_hi_done = sem("x_hi_done")
        x_split = sem("x_split")
        filled = [sem(f"filled{i}") for i in range(2)]
        freed = [sem(f"freed{i}") for i in range(2)]
        consts_act = sem("consts_act")
        dve_chain = sem("dve_chain")
        act_chain = sem("act_chain")
        roped = sem("roped")
        roped_hi = sem("roped_hi")
        roped_split = sem("roped_split")
        v_turned = sem("v_turned")
        v_hi_done = sem("v_hi_done")
        v_split = sem("v_split")
        silu_done = sem("silu_done")
        scores_done = sem("scores_done")
        scores_masked = sem("scores_masked")
        exp_done = sem("exp_done")
        probs_ready = sem("probs_ready")
        pt_done = sem("pt_done")
        pt_hi_done = sem("pt_hi_done")
        pt_split = sem("pt_split")
        pv_done = sem("pv_done")
        attn_gated = sem("attn_gated")
        attn_hi_done = sem("attn_hi_done")
        attn_split = sem("attn_split")
        spilled = [sem(f"spilled{i}") for i in range(2)]
        padding_zero = sem("padding_zero")
        conv_begun = sem("conv_begun")
        convolved = sem("convolved")
        conv_hi_done = sem("conv_hi_done")
        conv_split = sem("conv_split")
        conv_used = sem("conv_used")
        sigm_g_done = sem("sigm_g_done")
        gate_filled = [sem(f"gate_filled{i}") for i in range(2)]
        gate_freed = [sem(f"gate_freed{i}") for i in range(2)]
        squared = sem("squared")
        one_less = sem("one_less")
        rooted = sem("rooted")
        rnn_done = sem("rnn_done")
        rnn_hi_done = sem("rnn_hi_done")
        rnn_split = sem("rnn_split")
        attn_in_landed = sem("attn_in_landed")
        attn_in_used = sem("attn_in_used")
        merged_done = sem("merged_done")
        merged_hi_done = sem("merged_hi_done")
        merged_split = sem("merged_split")
        rows_landed = sem("rows_landed")
        ln_landed = sem("ln_landed")
        out_done = sem("out_done")
        out_added = sem("out_added")
        var_done = sem("var_done")
        root_done = sem("root_done")
        scaled_by = sem("scaled_by")
        normed = sem("normed")
        gained = sem("gained")
        shifted = sem("shifted")
        stored = sem("stored")
        pool_waited = sem("pool_waited")
        dve_waited = sem("dve_waited")
        pool_chain = sem("pool_chain")
        act_tanh = sem("act_tanh")
        act_decay = sem("act_decay")
        sink_placed = sem("sink_placed")
        rdenom_done = sem("rdenom_done")
        tap_done = sem("tap_done")
        u_done = sem("u_done")
        scanned = sem("scanned")
        mixed = sem("mixed")
        resid = sem("resid")
        stats_done = sem("stats_done")

        def bias(col):
            return par[:, ds(B_IN + col, 1)]

        def at_part(hi, head):
            t = (at_hi, at_hi2) if hi else (at_lo, at_lo2)
            return t[head // 2][:, (head % 2) * SEQ:(head % 2 + 1) * SEQ]

        def key_blocks(n):
            return list(range(max(n - 1, 0), min(n + 1, NB - 1) + 1))

        def pt_segments(n):
            runs = []
            for i, kb in enumerate(key_blocks(n)):
                slot = 3 * (kb % 4) + n - kb + 1
                if runs and slot == runs[-1][2] + 2 * runs[-1][1]:
                    runs[-1][1] += 1
                else:
                    runs.append([i, 1, slot])
            return runs

        SLICES = {1: 2, 2: 2, 3: 2, 4: 1, 5: 1, 6: 1, 7: 1, 8: 2, 9: 2, 10: 2}
        row_bank = [t[:, h * HALF:(h + 1) * HALF] for t in aux + buf for h in range(2)]

        block = ctx.enter_context(nc.Block())

        @block.sync
        def _(sp):
            def load(index, slot, col, cols=UNIT):
                sp.wait_ge(unit_split, index + 1)
                sp.dma_start(raw[:, slot, 0:cols], stream[:, ds(col, cols)]).then_inc(raw_landed[slot], 16)

            for n in range(2):
                load(n, n, n * UNIT)
                sp.dma_start(x_raw[:, n, :], x_t[:, n, :]).then_inc(x_landed[n], 16)
            for k in range(2, KT):
                sp.dma_start(x_raw[:, k, :], x_t[:, k, :]).then_inc(x_landed[k], 16)
            with sp.Fori(0, N_GROUPS) as g:
                for n in range(UNITS_GROUP):
                    load(g * UNITS_GROUP + 2 + n, n % 2, (g * UNITS_GROUP + 2 + n) * UNIT)
            at = COLS_B
            for n, cols in enumerate((HALF, UNIT, UNIT, HALF)):
                load(UNIT_B + n, n % 2, at, cols)
                at += cols
            with sp.Fori(0, PAIRS - 1) as p:
                at = COLS_P
                for n, cols in enumerate((UNIT, UNIT, HALF, UNIT) * 2):
                    load(p * UNITS_PAIR + UNIT_P + n, n % 2, p * COLS_PAIR + at, cols)
                    at += cols
            for n in range(2):
                load(UNIT_C + n, n, COLS_C + n * UNIT)
            for i in range(2):
                sp.wait_ge(spilled[i], 16 * (1 + 4 * N_GROUPS))
            sp.wait_ge(conv_used, RNN_BLOCKS + 1)
            sp.wait_ge(gate_filled[1], 2 * RNN_BLOCKS)

            def load_attn(d):
                sp.wait_ge(attn_in_used, d + 1)
                sp.dma_start(attn_in[:, :, :], spill[:, :, ds(d * SEQ, SEQ)]
                             .rearrange("g p s -> p g s")).then_inc(attn_in_landed, 16)

            load_attn(0)
            for n in range(2):
                load(UNIT_C + 2 + n, n, COLS_C + (2 + n) * UNIT)
            for first_d, count, unit, before in TILES_C:
                with sp.Fori(0, count) as i:
                    for n in range(2):
                        load(i * 2 + unit + n, n, i * (2 * UNIT) + COLS_C + (unit - UNIT_C + n) * UNIT)
                    load_attn(i + first_d)
                if before < 4:
                    for n in range(2):
                        load(UNIT_WO0[before // 2] + n, n, COLS_C + (UNIT_WO0[before // 2] - UNIT_C + n) * UNIT)
            for n in range(4):
                load(UNIT_WO1 + n, n % 2, COLS_C + (UNIT_WO1 - UNIT_C + n) * UNIT)
            sp.wait_ge(filled[0], FILL_D)
            sp.wait_ge(filled[1], FILL_D)
            for n in range(NB):
                sp.dma_start(rows[:, n, :], x_rows[n * P:(n + 1) * P, :]).then_inc(rows_landed, 16)
            sp.wait_ge(merged_split, KT + 1)
            for dst, src in ((bias_o, b_out), (gain, ln_gain), (shift, ln_bias)):
                sp.dma_start(dst[:, :], src.partition_broadcast(P)).then_inc(ln_landed, 16)
            for n in range(NB):
                sp.wait_ge(shifted, n + 1)
                sp.dma_start(out[n * P:(n + 1) * P, :], rows[:, n, :]).then_inc(stored, 16)
            sp.wait_ge(stored, 16 * NB)

        @block.gpsimd
        def _(pool):
            pool.sem_inc(unit_split, 2)

            def split(index, slot, cols, hi, lo, ring_index=None):
                pool.wait_ge(raw_landed[slot], (index - slot) * 8 + 16)
                if ring_index is not None:
                    pool.wait_ge(unit_begun, ring_index + 1)
                pool.sem_inc(pool_waited, 1)
                nc.gpsimd.tensor_scalar(hi, raw[:, slot, 0:cols], 1.0, 0.0, ALU.mult, ALU.add)\
                    .then_inc(pool_chain, 1)
                pool.wait_ge(pool_chain, index + 1)
                nc.gpsimd.tensor_tensor(lo, raw[:, slot, 0:cols], hi.bitcast(f32), ALU.subtract)\
                    .then_inc(unit_split, 1)

            def ring(index, slot, cols=UNIT, before=0):
                split(index, slot, cols, w_hi[:, slot, 0:cols], w_lo[:, slot, 0:cols], index - before)

            def output_weights(unit, count, hi, lo, k):
                for n in range(count):
                    split(unit + n, n % 2, UNIT, hi[:, k + 2 * n:k + 2 * n + 2, :].rearrange("p k c -> p (k c)"),
                          lo[:, k + 2 * n:k + 2 * n + 2, :].rearrange("p k c -> p (k c)"))

            for n in range(2):
                ring(n, n)
            with pool.Fori(0, N_GROUPS) as g:
                for n in range(UNITS_GROUP):
                    ring(g * UNITS_GROUP + 2 + n, n % 2)
            for n, cols in enumerate((HALF, UNIT, UNIT, HALF)):
                ring(UNIT_B + n, n % 2, cols)
            with pool.Fori(0, PAIRS - 1) as p:
                for n, cols in enumerate((UNIT, UNIT, HALF, UNIT) * 2):
                    ring(p * UNITS_PAIR + UNIT_P + n, n % 2, cols)
            for n in range(4):
                ring(UNIT_C + n, n % 2)
            for first_d, count, unit, before in TILES_C:
                with pool.Fori(0, count) as i:
                    for n in range(2):
                        ring(i * 2 + unit + n, n, before=before)
                if before < 4:
                    if before == 0:
                        pool.wait_ge(rnn_split, RNN_BLOCKS + 1)
                    output_weights(UNIT_WO0[before // 2], 2, wo0_hi, wo0_lo, 2 * before)
            pool.wait_ge(filled[0], FILL_D)
            pool.wait_ge(filled[1], FILL_D)
            output_weights(UNIT_WO1, 4, wo1_hi, wo1_lo, 0)
            pool.wait_ge(ln_landed, 48)
            for n in range(NB - 1):
                pool.wait_ge(gained, n + 1)
                nc.gpsimd.tensor_tensor(rows[:, n, :], rows[:, n, :], shift[:, :], ALU.add)\
                    .then_inc(shifted, 1)

        @block.tensor
        def _(pe):
            pe.sem_inc(unit_begun, 1)
            pe.sem_inc(scores_done, 1)
            pe.sem_inc(pt_done, 2)
            pe.sem_inc(pv_done, NB)

            def part_slice(slot, col, banks, mov_hi, mov_lo, first, last):
                wh, wl = w_hi[:, slot, col:col + P], w_lo[:, slot, col:col + P]
                begun = None
                for h in range(2):
                    i = nc.tensor.matmul(banks[:, h * HALF:(h + 1) * HALF], wh,
                                         mov_hi[:, h * HALF:(h + 1) * HALF], start=first, stop=False)
                    begun = begun or i
                    nc.tensor.matmul(banks[:, h * HALF:(h + 1) * HALF], wh,
                                     mov_lo[:, h * HALF:(h + 1) * HALF], start=False, stop=False)
                for h in range(2):
                    i = nc.tensor.matmul(banks[:, h * HALF:(h + 1) * HALF], wl,
                                         mov_hi[:, h * HALF:(h + 1) * HALF], start=False, stop=last)
                return begun, i

            def tile_slice(k, unit, slot, fill, b, wait_x=False):
                if k == 0:
                    pe.wait_ge(unit_split, unit + 3)
                    pe.wait_ge(freed[b], fill + 1)
                if wait_x:
                    pe.wait_ge(x_split, k + 1)
                first, last = part_slice(slot, k * P, buf[b], xt_hi[:, k, :], xt_lo[:, k, :],
                                         k == 0, k == KT - 1)
                if k == 0:
                    first.then_inc(unit_begun, 1)
                if k == KT - 1:
                    last.then_inc(filled[b], 1)

            def tile(unit, slot, fill, b, wait_x=False):
                for k in range(KT):
                    tile_slice(k, unit, slot, fill, b, wait_x)

            def scores(m, n):
                pe.wait_ge(scores_masked, m + n + 1)
                ks = key_blocks(n)
                q = slice(n * P, (n + 1) * P)
                keys = slice(ks[0] * P, (ks[-1] + 1) * P)
                dst = s_ps[:, 0:len(ks) * P]
                nc.tensor.matmul(dst, q_hi[:, q], k_hi[:, keys], start=True, stop=False)
                nc.tensor.matmul(dst, q_hi[:, q], k_lo[:, keys], start=False, stop=False)
                nc.tensor.matmul(dst, q_lo[:, q], k_hi[:, keys], start=False, stop=True)\
                    .then_inc(scores_done, 1)

            def transpose_probs(m, n):
                pe.wait_ge(probs_ready, m + n + 2)
                pe.wait_ge(pt_split, m + n + 1)
                nk = len(key_blocks(n))
                for i in range(nk):
                    at = (3 - nk + i) * P
                    last = nc.tensor.transpose(pt_ps[:, i * P:(i + 1) * P], probs[:, n % 2, at:at + P],
                                               table[:, T_IDENT:T_IDENT + P])
                last.then_inc(pt_done, 1)

            def weigh_values(head2, m, kb):
                pe.wait_ge(pt_split, m + min(kb + 1, NB - 1) + 2)
                if kb == 0:
                    pe.wait_ge(attn_gated, head2 + 1)
                if kb == NB // 2 - 1:
                    pe.wait_ge(attn_gated, head2 + 2)
                lo, hi = max(kb - 1, 0), min(kb + 1, NB - 1)
                half = NB // 2
                runs = [(a, z) for a, z in ((lo, min(hi, half - 1)), (max(lo, half), hi)) if a <= z]
                for v, p in ((v_hi, pt_hi), (v_hi, pt_lo), (v_lo, pt_hi)):
                    for a, z in runs:
                        slot = 3 * (kb % 4) + a - kb + 1
                        opens = v is v_hi and p is pt_hi and ((a == 0 and kb == 0) or (a == half and kb == half - 1))
                        last = nc.tensor.matmul(
                            ot_ps[:, a * P:(z + 1) * P], v[:, kb * P:(kb + 1) * P],
                            p[:, slot:slot + z - a + 1, :].rearrange("p n c -> p (n c)"),
                            start=opens, stop=v is v_lo, skip_group_check=True)
                last.then_inc(pv_done, 1)

            def attention(g, h, unit, fill, more):
                m = h * NB + g * HEADS * NB
                at = 0
                for n in range(1, NB + 3):
                    if n < NB:
                        scores(m, n)
                    if n == NB + 2 and more:
                        pe.wait_ge(roped_split, h + g * (HEADS + 1) + 4)
                        scores(m + NB, 0)
                    share = SLICES[n]
                    for i in range(share):
                        if i == share // 2 and n <= NB:
                            transpose_probs(m, n - 1)
                        b, k = divmod(at, KT)
                        tile_slice(k, unit + b, b, fill, b)
                        at += 1
                    if n >= 3:
                        if n == 3:
                            pe.wait_ge(v_split, g + 1)
                        weigh_values(h * 2 + g * 2 * HEADS, m, n - 3)

            for b in range(2):
                tile(b, b, 0, b, wait_x=b == 0)
            for g in range(N_GROUPS):
                unit, fill = 2 + g * UNITS_GROUP, 1 + g * FILLS_GROUP
                tile(unit, 0, fill, 0)
                pe.wait_ge(freed[1], fill + 1)
                pe.wait_ge(table_landed, 16)
                pe.wait_ge(attn_gated, g * 2 * HEADS + 2)
                for n in range(NB):
                    last = nc.tensor.transpose(ot_ps[:, n * P:(n + 1) * P], tanh_g[:, n * P:(n + 1) * P],
                                               table[:, T_IDENT:T_IDENT + P])
                last.then_inc(v_turned, 1)
                tile(unit + 1, 1, fill, 1)
                pe.wait_ge(roped_split, g * (HEADS + 1) + 3)
                scores(g * HEADS * NB, 0)
                with pe.Fori(0, HEADS - 1) as h:
                    attention(g, h, h * 2 + (unit + 2), h + (fill + 1), True)
                attention(g, HEADS - 1, unit + 2 * HEADS, fill + HEADS, False)
                for n in range(KT // 2):
                    pe.wait_ge(unit_split, unit + 2 + 2 * HEADS + n + 3)
                    for b in range(2):
                        pe.wait_ge(freed[b], fill + HEADS + 1 + n + 1)
                        for k in range(HEADS):
                            pe.wait_ge(attn_split, g * (2 * HEADS) + 2 * (k + 1) + 2)
                            first, last = part_slice(n % 2, (b * HEADS + k) * P, buf[b],
                                                     at_hi[:, k * SEQ:(k + 1) * SEQ],
                                                     at_lo[:, k * SEQ:(k + 1) * SEQ], k == 0, k == HEADS - 1)
                            if b == 0 and k == 0:
                                first.then_inc(unit_begun, 1)
                        last.then_inc(filled[b], 1)

            def gates(unit, slot, b_index):
                pe.wait_ge(unit_split, unit + 3)
                pe.wait_ge(conv_split, b_index + 1)
                for n in range(4):
                    a = n % 2
                    pe.wait_ge(gate_freed[a], b_index * 2 + n // 2 + 1)
                    first, last = part_slice(slot, n * P, aux[a], conv_hi, conv_lo, True, True)
                    if n == 0:
                        first.then_inc(unit_begun, 1)
                    last.then_inc(gate_filled[a], 1)

            def rnn_branch(unit, slot, fill, pair):
                pe.wait_ge(unit_split, unit + 3)
                for j in range(4):
                    b = j % 2
                    pe.wait_ge(freed[b], fill + j // 2 + 1)
                    for k in range(2):
                        first, last = part_slice(slot, (2 * j + k) * P, buf[b], h_hi[pair][:, k, :],
                                                 h_lo[pair][:, k, :], k == 0, k == 1)
                        if j == 0 and k == 0:
                            first.then_inc(unit_begun, 1)
                    last.then_inc(filled[b], 1)

            pe.wait_ge(scores_masked, N_HEADS * NB + 1)
            pe.wait_ge(pt_split, N_HEADS * NB + 1)
            pe.wait_ge(attn_gated, 2 * N_HEADS + 2)
            gates(UNIT_B, 0, 0)
            tile(UNIT_B + 1, 1, FILL_B, 0)
            tile(UNIT_B + 2, 0, FILL_B, 1)
            gates(UNIT_B + 3, 1, 1)
            with pe.Fori(0, (PAIRS - 1) // 2) as pp:
                for i in range(2):
                    for j in range(2):
                        u = pp * (2 * UNITS_PAIR) + UNIT_P + i * UNITS_PAIR + 4 * j
                        f = pp * (2 * FILLS_PAIR) + FILL_P + i * FILLS_PAIR + 3 * j
                        b_index = pp * 4 + 2 + 2 * i + j
                        tile(u, 0, f, 0)
                        tile(u + 1, 1, f, 1)
                        gates(u + 2, 0, b_index)
                        if j == 0:
                            pe.wait_ge(rnn_split, b_index + 1)
                        rnn_branch(u + 3, 1, f + 1, i)

            tile(UNIT_C, 0, FILL_C, 0)
            tile(UNIT_C + 1, 1, FILL_C, 1)
            pe.wait_ge(rnn_split, RNN_BLOCKS + 1)
            for n in range(2):
                rnn_branch(UNIT_C + 2 + n, n, FILL_C + 1 + 2 * n, (PAIRS - 1) % 2)
            for first_d, count, unit, before in TILES_C:
                with pe.Fori(0, count) as i:
                    tile(i * 2 + unit, 0, i + (FILL_C + 4 + first_d), 0)
                    tile(i * 2 + unit + 1, 1, i + (FILL_C + 4 + first_d), 1)

            def rows_slice(n, half, k):
                wh, wl = ((wo0_hi, wo0_lo), (wo1_hi, wo1_lo))[half]
                s = slice(n * P, (n + 1) * P)
                nc.tensor.matmul(row_bank[n], merged_hi[:, k, s], wh[:, k, :], start=k == 0, stop=False)
                nc.tensor.matmul(row_bank[n], merged_hi[:, k, s], wl[:, k, :], start=False, stop=False)
                last = nc.tensor.matmul(row_bank[n], merged_lo[:, k, s], wh[:, k, :],
                                        start=False, stop=k == KT - 1)
                if k == KT - 1:
                    last.then_inc(out_done, 1)

            pe.wait_ge(gate_freed[0], 2 * RNN_BLOCKS + 1)
            pe.wait_ge(gate_freed[1], 2 * RNN_BLOCKS + 1)
            pe.wait_ge(unit_split, UNIT_WO0[1] + 2 + 2)
            pe.wait_ge(merged_split, KT)
            for n in range(NB // 2):
                for k in range(KT - 1):
                    rows_slice(n, 0, k)
            pe.wait_ge(merged_split, KT + 1)
            for n in range(NB // 2):
                rows_slice(n, 0, KT - 1)
            pe.wait_ge(freed[0], FILL_D + 1)
            pe.wait_ge(freed[1], FILL_D + 1)
            for n in range(NB // 2, NB):
                for k in range(KT):
                    rows_slice(n, 0, k)
            pe.wait_ge(unit_split, UNIT_WO1 + 4 + 2)
            for n in range(NB):
                pe.wait_ge(out_added, n + 1)
                for k in range(KT):
                    rows_slice(n, 1, k)

        @block.scalar
        def _(act):
            for s, credit in ((exp_done, 1), (gate_freed[0], 1), (gate_freed[1], 1),
                              (spilled[0], 16), (spilled[1], 16), (freed[1], 1)):
                act.sem_inc(s, credit)
            act.dma_start(par[:, :], small).then_inc(small_landed, 16)
            act.dma_start(nsink[:, :], sink.partition_broadcast(P)).then_inc(small_landed, 16)
            act.dma_start(table[:, :], tables).then_inc(table_landed, 16)

            def copy(dst, src):
                return nc.scalar.activation(dst, src, ACT.Copy)

            for k in range(KT):
                act.wait_ge(x_landed[k], 16)
                copy(xt_hi[:, k, :], x_raw[:, k, :]).then_inc(x_hi_done, 1)
            act.wait_ge(small_landed, 32)
            nc.scalar.activation(half_b[:, :], par[:, B_IN:B_IN + B_RNN], ACT.Copy, scale=0.5)\
                .then_inc(act_chain, 1)
            nc.scalar.activation(nrate[:, :], par[:, LAMBDA:LAMBDA + 2 * RNN_BLOCKS], ACT.Abs)\
                .then_inc(act_chain, 1)
            act.wait_ge(act_chain, 2)
            nc.scalar.activation(nrate[:, :], nrate[:, :], ACT.Exp, scale=-1.0).then_inc(consts_act, 1)

            def v_evac(g, fill, col):
                act.wait_ge(filled[1], fill + 1)
                act.wait_ge(silu_done, g * HEADS + 1)
                nc.scalar.activation(tanh_g[:, :], buf[1][:, :], ACT.Identity, bias=bias(col))\
                    .then_inc(freed[1], 1)

            def gate_evac(g, h):
                col = h * 2 + (g * (2 + 2 * HEADS) + 3)
                act.wait_ge(filled[1], h + (g * FILLS_GROUP + 2))
                act.wait_ge(attn_gated, h * 2 + (g * 2 * HEADS + 2))
                act.wait_ge(silu_done, h + (g * HEADS + 1))
                nc.scalar.activation(gate[:, :], buf[1][:, :], ACT.Identity, scale=0.5,
                                     bias=half_b[:, ds(col, 1)])
                nc.scalar.activation(tanh_g[:, :], buf[1][:, :], ACT.Tanh, scale=0.5,
                                     bias=half_b[:, ds(col, 1)]).then_inc(freed[1], 1)

            def rope_hi(dst, count, last_scores):
                act.wait_ge(roped, count)
                act.wait_ge(scores_done, last_scores + 1)
                copy(dst[:, :], rot_a[:, :]).then_inc(roped_hi, 1)

            def exponentials(m, n):
                c0 = (3 - len(key_blocks(n))) * P
                act.wait_ge(pt_done, m + n + 1)
                act.wait_ge(scores_masked, m + n + 2)
                nc.scalar.activation(probs[:, n % 2, c0:3 * P + 1], masked[:, c0:3 * P + 1],
                                     ACT.Exp, scale=-1.0, bias=neg_max[:, 0:1],
                                     accum_out=denom[:, 0:1]).then_inc(exp_done, 1)

            def attention_hi(g, h, half):
                act.wait_ge(attn_gated, h * 2 + (g * 2 * HEADS + half + 3))
                copy(at_hi[:, ds(h * SEQ + half * HALF, HALF)], gated[:, half * HALF:(half + 1) * HALF])\
                    .then_inc(attn_hi_done, 1)

            def attention(g, h, next_rope, more):
                m = h * NB + g * HEADS * NB
                for n in range(1, NB + 3):
                    if n < NB:
                        exponentials(m, n)
                    if n <= NB:
                        q = n - 1
                        act.wait_ge(pv_done, m + min(q, NB - 2) + 6)
                        act.wait_ge(pt_done, m + q + 3)
                        for i, count, slot in pt_segments(q):
                            last = copy(pt_hi[:, slot:slot + 2 * count - 1:2, :],
                                        pt_ps[:, i * P:(i + count) * P].rearrange("p (n c) -> p n c", c=P))
                        last.then_inc(pt_hi_done, 1)
                    if n == 2:
                        gate_evac(g, h)
                    if n == NB + 1:
                        if next_rope is not None:
                            rope_hi(next_rope, h + (g * (HEADS + 1) + 3), m + NB)
                        attention_hi(g, h, 0)
                    if n == NB + 2 and more:
                        exponentials(m + NB, 0)
                attention_hi(g, h, 1)

            def block_head(b, fill):
                act.wait_ge(padding_zero, 1)
                act.wait_ge(convolved, b + 1)
                act.wait_ge(filled[0], fill + 1)
                nc.scalar.activation(padded[:, CONV_LEFT:CONV_LEFT + SEQ], buf[0][:, :], ACT.Identity,
                                     bias=bias(b * 2 + B_RNN)).then_inc(freed[0], 1)
                act.wait_ge(freed[0], fill + 2)
                act.wait_ge(conv_used, b + 1)
                nc.scalar.activation(conv[:, :], padded[:, 0:SEQ], ACT.Identity,
                                     scale=par[:, ds(b + CONV_WEIGHT, 1)],
                                     bias=par[:, ds(b + CONV_BIAS, 1)]).then_inc(conv_begun, 1)
                act.wait_ge(convolved, b + 2)
                copy(conv_hi[:, :], conv[:, :]).then_inc(conv_hi_done, 1)
                act.wait_ge(rnn_split, b + 1)
                act.wait_ge(filled[1], fill + 1)
                nc.scalar.activation(silu_g[:, :], buf[1][:, :], ACT.Sigmoid,
                                     bias=bias(b * 2 + B_RNN + 1)).then_inc(sigm_g_done, 1)

            def block_tail(b, pair, j):
                for n, (dst, first) in enumerate(((decay, GATE_A), (state, GATE_X))):
                    for d in range(2):
                        act.wait_ge(gate_filled[d], b * 2 + n + 1)
                        nc.scalar.activation(dst[d][:, :], aux[d][:, :], ACT.Sigmoid,
                                             bias=par[:, ds(b + first + d * RNN_BLOCKS, 1)])\
                            .then_inc(gate_freed[d], 1)
                for d in range(2):
                    act.wait_ge(gate_freed[d], b * 2 + 2)
                    nc.scalar.activation(root[d][:, :], decay[d][:, :], ACT.Tanh,
                                         scale=rate[:, ds(b + d * RNN_BLOCKS, 1)]).then_inc(act_tanh, 1)
                act.wait_ge(act_tanh, b * 2 + 2)
                for d in range(2):
                    nc.scalar.activation(decay[d][:, :], decay[d][:, :], ACT.Exp,
                                         scale=nrate[:, ds(b + d * RNN_BLOCKS, 1)]).then_inc(act_decay, 1)
                for d in range(2):
                    act.wait_ge(act_decay, b * 2 + d + 1)
                    if d == 1:
                        act.wait_ge(one_less, b * 2 + 1)
                    nc.scalar.activation(square[:, :], decay[d][:, :], ACT.Square).then_inc(squared, 1)
                for d in range(2):
                    act.wait_ge(one_less, b * 2 + d + 1)
                    nc.scalar.activation(root[d][:, :], root[d][:, :], ACT.Sqrt).then_inc(rooted, 1)
                act.wait_ge(rnn_done, b + 1)
                copy(h_hi[pair][:, j, :], state[0][:, :]).then_inc(rnn_hi_done, 1)

            rope_hi(k_hi, 1, 0)
            v_evac(0, 0, 1)
            for g in range(N_GROUPS):
                rope_hi(q_hi, g * (HEADS + 1) + 2, g * HEADS * NB)
                act.wait_ge(v_turned, g + 1)
                act.wait_ge(pv_done, g * HEADS * NB + NB)
                copy(v_hi[:, :], ot_ps[:, :]).then_inc(v_hi_done, 1)
                exponentials(g * HEADS * NB, 0)
                with act.Fori(0, HEADS - 1) as h:
                    attention(g, h, q_hi, True)
                attention(g, HEADS - 1, k_hi if g < N_GROUPS - 1 else None, False)
                if g < N_GROUPS - 1:
                    v_evac(g + 1, g * FILLS_GROUP + HEADS + 1, (g + 1) * (2 + 2 * HEADS) + 1)
                else:
                    block_head(0, FILL_X0)
                for n in range(KT // 2):
                    for b in range(2):
                        fill = (g + 1) * FILLS_GROUP - 3 + n
                        act.wait_ge(spilled[b], g * (16 * KT // 2) + 16 * (n + 1))
                        act.wait_ge(filled[b], fill + 1)
                        copy(part[:, b, :], buf[b][:, :]).then_inc(freed[b], 1)
                        act.wait_ge(freed[b], fill + 2)
                        act.dma_start(spill[g, :, (2 * n + b) * SEQ:(2 * n + b + 1) * SEQ], part[:, b, :])\
                            .then_inc(spilled[b], 16)

            act.wait_ge(filled[0], FILL_B)
            act.wait_ge(filled[1], FILL_B)
            act.wait_ge(attn_split, 2 * N_HEADS + 2)
            for i in range(2):
                act.wait_ge(spilled[i], 16 * (1 + 4 * N_GROUPS))
            block_tail(0, 0, 0)
            block_head(1, FILL_B)
            block_tail(1, 0, 1)
            with act.Fori(0, (PAIRS - 1) // 2) as pp:
                for i in range(2):
                    for j in range(2):
                        b = pp * 4 + 2 + 2 * i + j
                        block_head(b, pp * (2 * FILLS_PAIR) + FILL_P + i * FILLS_PAIR + 3 * j)
                        block_tail(b, 1 - i, j)

            act.wait_ge(convolved, RNN_BLOCKS + 1)
            act.wait_ge(conv_used, RNN_BLOCKS + 1)

            def merge(d, fill):
                act.wait_ge(merged_split, d + 1)
                for b, dst in enumerate((gate_a, gate_r)):
                    act.wait_ge(filled[b], fill + 1)
                    nc.scalar.activation(dst[:, :], buf[b][:, :], ACT.Sigmoid,
                                         bias=bias(d * 2 + B_MERGE + b)).then_inc(freed[b], 1)
                act.wait_ge(merged_done, d + 1)
                copy(merged_hi[:, ds(d, 1), :].rearrange("p k s -> p (k s)"), gate_a[:, :])\
                    .then_inc(merged_hi_done, 1)

            merge(0, FILL_C)
            for first_d, count, _, _ in TILES_C:
                with act.Fori(0, count) as i:
                    merge(i + first_d, i + (FILL_C + 4 + first_d))

            for n in range(NB):
                act.wait_ge(var_done, n + 1)
                nc.scalar.activation(norm[:, n, 1:2], norm[:, n, 0:1], ACT.Sqrt).then_inc(root_done, 1)
                act.wait_ge(scaled_by, n + 1)
                nc.scalar.activation(rows[:, n, :], rows[:, n, :], ACT.Identity, scale=norm[:, n, 2:3],
                                     bias=norm[:, n, 3:4]).then_inc(normed, 1)

        @block.vector
        def _(dve):
            for s, credit in ((freed[0], 1), (roped_split, 1), (probs_ready, 1), (attn_split, 2), (silu_done, 1),
                              (scores_masked, 1), (pt_split, 1),
                              (attn_gated, 2), (convolved, 1), (conv_used, 1), (rnn_split, 1),
                              (attn_in_used, 1), (merged_split, 1)):
                dve.sem_inc(s, credit)

            def tt(dst, a, b, op):
                return nc.vector.tensor_tensor(dst, a, b, op)

            def stt(dst, a, scalar, b, op0, op1):
                return nc.vector.scalar_tensor_tensor(dst, a, scalar, b, op0, op1)

            steps = [0]

            def link(ins):
                steps[0] += 1
                ins.then_inc(dve_chain, 1)
                dve.wait_ge(dve_chain, steps[0])

            for k in range(KT):
                dve.wait_ge(x_hi_done, k + 1)
                tt(xt_lo[:, k, :], x_raw[:, k, :], xt_hi[:, k, :].bitcast(f32), ALU.subtract)\
                    .then_inc(x_split, 1)
            dve.wait_ge(small_landed, 32)
            link(nc.vector.tensor_scalar(nsink[:, :], nsink[:, :], -1.0, None, ALU.mult))
            dve.wait_ge(consts_act, 1)
            e, s, s2 = nrate[:, :], norm_scratch[:, 0, :], norm_scratch[:, 1, :]
            acc = norm_scratch[:, 2, :]
            link(nc.vector.tensor_scalar(s, e, 2.0, None, ALU.add))
            link(nc.vector.reciprocal(s, s))
            link(tt(s, s, e, ALU.mult))
            link(tt(s2, s, s, ALU.mult))
            link(nc.vector.tensor_scalar(acc, s2, 1.0 / 19, None, ALU.mult))
            for odd in range(17, 1, -2):
                link(stt(acc, acc, 1.0 / odd, s2, ALU.add, ALU.mult))
            link(stt(acc, acc, 1.0, s, ALU.add, ALU.mult))
            link(nc.vector.tensor_scalar(s, par[:, LAMBDA:LAMBDA + 2 * RNN_BLOCKS], -1.0, 0.0,
                                         ALU.mult, ALU.max))
            link(stt(s, acc, 2.0, s, ALU.mult, ALU.add))
            link(nc.vector.tensor_scalar(rate[:, :], s, LRU_C, None, ALU.mult))
            link(nc.vector.tensor_scalar(nrate[:, :], s, -LRU_C, None, ALU.mult))
            dve.wait_ge(table_landed, 16)

            cos, sin = table[:, T_COS:T_COS + SEQ], table[:, T_SIN:T_SIN + SEQ]

            def rope(part, fill, col, count):
                if part == 0:
                    dve.wait_ge(filled[0], fill + 1)
                    dve.wait_ge(roped_split, count)
                    stt(rot_a[:, :], buf[0][:, :], bias(col), cos, ALU.add, ALU.mult)
                elif part == 1:
                    stt(rot_b[0:64, :], buf[0][64:P, :], par[64:P, ds(B_IN + col, 1)], sin[64:P, :],
                        ALU.add, ALU.mult)
                    stt(rot_b[64:P, :], buf[0][0:64, :], par[0:64, ds(B_IN + col, 1)], sin[0:64, :],
                        ALU.add, ALU.mult).then_inc(freed[0], 1)
                else:
                    dve.wait_ge(freed[0], fill + 2)
                    tt(rot_a[:, :], rot_a[:, :], rot_b[:, :], ALU.add).then_inc(roped, 1)

            def rope_lo(dst, hi, count):
                dve.wait_ge(roped_hi, count)
                tt(dst[:, :], rot_a[:, :], hi[:, :].bitcast(f32), ALU.subtract).then_inc(roped_split, 1)

            def silu(g, h):
                dve.wait_ge(freed[1], h + (g * FILLS_GROUP + 3))
                stt(gate[:, :], tanh_g[:, :], 1.0, gate[:, :], ALU.add, ALU.mult).then_inc(silu_done, 1)

            def gate_half(g, h, half):
                c = slice(half * HALF, (half + 1) * HALF)
                dve.wait_ge(silu_done, h + (g * HEADS + 2))
                dve.wait_ge(attn_split, h * 2 + (g * 2 * HEADS + half + 1))
                dve.wait_ge(pv_done, h * NB + (g * HEADS * NB + NB + (NB // 2 + 1, NB)[half]))
                tt(gated[:, c], ot_ps[:, c], gate[:, c], ALU.mult).then_inc(attn_gated, 1)

            def attention_lo(g, h, half):
                at = ds(h * SEQ + half * HALF, HALF)
                dve.wait_ge(attn_hi_done, h * 2 + (g * 2 * HEADS + half + 1))
                tt(at_lo[:, at], gated[:, half * HALF:(half + 1) * HALF], at_hi[:, at].bitcast(f32),
                   ALU.subtract).then_inc(attn_split, 1)

            def place_sink(g, h):
                dve.wait_ge(exp_done, h * NB + (g * HEADS * NB + 1))
                for dst in (masked[:, 3 * P:3 * P + 1], nsink_now[:, :]):
                    nc.vector.tensor_copy(dst, nsink[:, ds(h + g * HEADS, 1)]).then_inc(sink_placed, 1)
                dve.wait_ge(sink_placed, h * 2 + (g * 2 * HEADS + 2))

            def mask_scores(m, n):
                nk = len(key_blocks(n))
                c0 = (3 - nk) * P
                m0 = T_MASK + (0 if n else P)
                dve.wait_ge(exp_done, m + n + 1)
                dve.wait_ge(scores_done, m + n + 2)
                dve.sem_inc(dve_waited, 1)
                nc.vector.tensor_tensor_reduce(
                    out=masked[:, c0:3 * P], in0=s_ps[:, 0:nk * P], in1=table[:, m0:m0 + nk * P],
                    scale=-SCALE, scalar=nsink_now[:, 0:1], op0=ALU.add, op1=ALU.min,
                    accum_out=neg_max[:, 0:1]).then_inc(scores_masked, 1)

            def normalize(m, n):
                c0 = (3 - len(key_blocks(n))) * P
                dve.wait_ge(exp_done, m + n + 2)
                dve.wait_ge(probs_ready, m + n + 1)
                nc.vector.reciprocal(rdenom[:, :], denom[:, :]).then_inc(rdenom_done, 1)
                dve.wait_ge(rdenom_done, m + n + 1)
                nc.vector.tensor_scalar(probs[:, n % 2, c0:3 * P], probs[:, n % 2, c0:3 * P],
                                        rdenom[:, 0:1], None, ALU.mult).then_inc(probs_ready, 1)

            def attention(g, h, next_lo, next_hi, more):
                m = h * NB + g * HEADS * NB
                turn = (h + (g * FILLS_GROUP + 2), h * 2 + (g * (2 + 2 * HEADS) + 4),
                        h + (g * (HEADS + 1) + 3))
                if next_lo is k_lo:
                    turn = (turn[0], (g + 1) * (2 + 2 * HEADS), turn[2])
                for n in range(1, NB + 3):
                    if n < NB:
                        mask_scores(m, n)
                        normalize(m, n)
                    if n <= NB:
                        q = n - 1
                        dve.wait_ge(pt_hi_done, m + q + 1)
                        for i, count, slot in pt_segments(q):
                            at = slice(slot, slot + 2 * count - 1, 2)
                            last = tt(pt_lo[:, at, :],
                                      pt_ps[:, i * P:(i + count) * P].rearrange("p (n c) -> p n c", c=P),
                                      pt_hi[:, at, :].bitcast(f32), ALU.subtract)
                        last.then_inc(pt_split, 1)
                    if n == 3:
                        silu(g, h)
                    if NB - 2 <= n <= NB and next_lo is not None:
                        rope(n - NB + 2, *turn)
                    if n == NB + 1:
                        gate_half(g, h, 0)
                        if next_lo is not None:
                            rope_lo(next_lo, next_hi, turn[2])
                        attention_lo(g, h, 0)
                    if n == NB + 2:
                        if more:
                            place_sink(g, h + 1)
                            mask_scores(m + NB, 0)
                        gate_half(g, h, 1)
                        if more:
                            normalize(m + NB, 0)
                        attention_lo(g, h, 1)

            for part in range(3):
                rope(part, 0, 0, 1)
            rope_lo(k_lo, k_hi, 1)
            for g in range(N_GROUPS):
                for part in range(3):
                    rope(part, 1 + g * FILLS_GROUP, g * (2 + 2 * HEADS) + 2, g * (HEADS + 1) + 2)
                rope_lo(q_lo, q_hi, g * (HEADS + 1) + 2)
                dve.wait_ge(v_hi_done, g + 1)
                tt(v_lo[:, :], ot_ps[:, :], v_hi[:, :].bitcast(f32), ALU.subtract).then_inc(v_split, 1)
                place_sink(g, 0)
                mask_scores(g * HEADS * NB, 0)
                normalize(g * HEADS * NB, 0)
                with dve.Fori(0, HEADS - 1) as h:
                    attention(g, h, q_lo, q_hi, True)
                attention(g, HEADS - 1, *((k_lo, k_hi) if g < N_GROUPS - 1 else (None, None)), False)

            dve.wait_ge(scores_done, N_HEADS * NB + 1)
            dve.wait_ge(pv_done, N_HEADS * NB + NB)
            link(nc.vector.memset(padded[:, 0:CONV_LEFT], 0.0))
            nc.vector.memset(padded[:, CONV_LEFT + SEQ:CONV_W + SEQ], 0.0).then_inc(padding_zero, 1)
            dve.wait_ge(padding_zero, 1)

            def block_head(b, fill):
                dve.wait_ge(conv_begun, b + 1)
                for tap in range(1, CONV_W):
                    last = stt(conv[:, :], padded[:, tap:tap + SEQ],
                               par[:, ds(b + CONV_WEIGHT + tap * RNN_BLOCKS, 1)], conv[:, :],
                               ALU.mult, ALU.add)
                    if tap < CONV_W - 1:
                        last.then_inc(tap_done, 1)
                        dve.wait_ge(tap_done, b * (CONV_W - 2) + tap)
                last.then_inc(convolved, 1)
                dve.wait_ge(conv_hi_done, b + 1)
                tt(conv_lo[:, :], conv[:, :], conv_hi[:, :].bitcast(f32), ALU.subtract)\
                    .then_inc(conv_split, 1)
                dve.wait_ge(sigm_g_done, b + 1)
                stt(silu_g[:, :], buf[1][:, :], bias(b * 2 + B_RNN + 1), silu_g[:, :], ALU.add, ALU.mult)\
                    .then_inc(freed[1], 1)

            def block_tail(b, pair, j, add):
                for d in range(2):
                    dve.wait_ge(gate_freed[d], b * 2 + 3)
                    last = tt(state[d][:, :], state[d][:, :], conv[:, :], ALU.mult)
                last.then_inc(conv_used, 1)
                add(0)
                add(1)
                for d in range(2):
                    dve.wait_ge(squared, b * 2 + d + 1)
                    stt(root[d][:, :], square[:, :], 1.0, root[d][:, :], ALU.add, ALU.mult)\
                        .then_inc(one_less, 1)
                    add(2 + d)
                dve.wait_ge(conv_used, b + 2)
                for d in range(2):
                    dve.wait_ge(rooted, b * 2 + d + 1)
                    tt(state[d][:, :], state[d][:, :], root[d][:, :], ALU.mult).then_inc(u_done, 1)
                for d, turn in ((0, 1), (1, -1)):
                    dve.wait_ge(u_done, b * 2 + d + 1)
                    last = nc.vector.tensor_tensor_scan(state[d][:, ::turn], decay[d][:, ::turn],
                                                        state[d][:, ::turn], 0.0, ALU.mult, ALU.add)
                last.then_inc(scanned, 1)
                dve.wait_ge(scanned, b * 2 + 1)
                tt(state[0][:, :], state[0][:, :], state[1][:, :], ALU.add).then_inc(scanned, 1)
                dve.wait_ge(scanned, b * 2 + 2)
                tt(state[0][:, :], state[0][:, :], silu_g[:, :], ALU.mult).then_inc(rnn_done, 1)
                dve.wait_ge(rnn_hi_done, b + 1)
                tt(h_lo[pair][:, j, :], state[0][:, :], h_hi[pair][:, j, :].bitcast(f32), ALU.subtract)\
                    .then_inc(rnn_split, 1)

            def add_branch(d, fill):
                b = d % 2
                dve.wait_ge(filled[b], fill + 1)
                tt(racc[:, d, :], buf[b][:, :], racc[:, d, :], ALU.add).then_inc(freed[b], 1)

            def nothing(n):
                return None

            block_head(0, FILL_X0)
            dve.wait_ge(filled[0], FILL_B)
            dve.wait_ge(filled[1], FILL_B)
            for i in range(2):
                dve.wait_ge(spilled[i], 16 * (1 + 4 * N_GROUPS))
            link(nc.vector.memset(racc[:, :, :], 0.0))
            block_tail(0, 0, 0, nothing)
            block_head(1, FILL_B)
            block_tail(1, 0, 1, nothing)
            with dve.Fori(0, (PAIRS - 1) // 2) as pp:
                for i in range(2):
                    for j in range(2):
                        b = pp * 4 + 2 + 2 * i + j
                        f = pp * (2 * FILLS_PAIR) + FILL_P + i * FILLS_PAIR + 3 * j
                        block_head(b, f)
                        block_tail(b, 1 - i, j, lambda n: add_branch(4 * j + n, f + 1 + n // 2))
            for d in range(KT):
                add_branch(d, FILL_C + 1 + d // 2)

            def merge(d, fill):
                dve.wait_ge(attn_in_landed, d * 16 + 16)
                tt(attn_in[:, 0, :], attn_in[:, 0, :], attn_in[:, 1, :], ALU.add).then_inc(mixed, 1)
                dve.wait_ge(freed[1], fill + 2)
                tt(gate_r[:, :], gate_r[:, :], racc[:, ds(d, 1), :].rearrange("p k s -> p (k s)"),
                   ALU.mult)
                dve.wait_ge(mixed, d + 1)
                tt(gate_a[:, :], gate_a[:, :], attn_in[:, 0, :], ALU.mult).then_inc(attn_in_used, 1)
                dve.wait_ge(attn_in_used, d + 2)
                tt(gate_a[:, :], gate_a[:, :], gate_r[:, :], ALU.add).then_inc(merged_done, 1)
                dve.wait_ge(merged_hi_done, d + 1)
                tt(merged_lo[:, ds(d, 1), :].rearrange("p k s -> p (k s)"), gate_a[:, :],
                   merged_hi[:, ds(d, 1), :].rearrange("p k s -> p (k s)").bitcast(f32),
                   ALU.subtract).then_inc(merged_split, 1)

            merge(0, FILL_C)
            for first_d, count, _, _ in TILES_C:
                with dve.Fori(0, count) as i:
                    merge(i + first_d, i + (FILL_C + 4 + first_d))

            dve.wait_ge(rows_landed, 16 * NB)
            dve.wait_ge(ln_landed, 48)
            for n in range(NB):
                stt(rows[:, n, :], rows[:, n, :], ALPHA, bias_o[:, :], ALU.mult, ALU.add)\
                    .then_inc(resid, 1)
            for half in range(2):
                c = slice(half * HALF, (half + 1) * HALF)
                for n in range(NB):
                    dve.wait_ge(resid, n + 1)
                    dve.wait_ge(out_done, half * NB + n + 1)
                    tt(rows[:, n, c], row_bank[n], rows[:, n, c], ALU.add).then_inc(out_added, 1)
                    dve.wait_ge(out_added, half * NB + n + 1)
                    nc.vector.bn_stats(stats[:, n, half, :], rows[:, n, c]).then_inc(stats_done, 1)
                    if half:
                        dve.wait_ge(stats_done, NB + n + 1)
                        link(nc.vector.bn_aggr(moments[:, n, :], stats[:, n, :, :].rearrange("p a b -> p (a b)")))
                        nc.vector.tensor_scalar(norm[:, n, 0:1], moments[:, n, 1:2], LN_EPS, None, ALU.add)\
                            .then_inc(var_done, 1)
                        if n:
                            dve.wait_ge(normed, n)
                            tt(rows[:, n - 1, :], rows[:, n - 1, :], gain[:, :], ALU.mult).then_inc(gained, 1)
                        dve.wait_ge(root_done, n + 1)
                        link(nc.vector.reciprocal(norm[:, n, 2:3], norm[:, n, 1:2]))
                        stt(norm[:, n, 3:4], moments[:, n, 0:1], -1.0, norm[:, n, 2:3], ALU.mult, ALU.mult)\
                            .then_inc(scaled_by, 1)
            dve.wait_ge(normed, NB)
            tt(rows[:, NB - 1, :], rows[:, NB - 1, :], gain[:, :], ALU.mult).then_inc(gained, 1)
            dve.wait_ge(gained, NB)
            dve.wait_ge(shifted, NB - 1)
            tt(rows[:, NB - 1, :], rows[:, NB - 1, :], shift[:, :], ALU.add).then_inc(shifted, 1)


def _tables():
    half = HEAD_DIM // 2
    inv = (np.float32(ROPE_THETA) ** (-np.arange(half, dtype=np.float32) * np.float32(2.0 / HEAD_DIM)))
    ang = inv.astype(np.float32)[:, None] * np.arange(SEQ, dtype=np.float32)[None, :]
    cos, sin = np.cos(ang).astype(np.float32), np.sin(ang).astype(np.float32)
    q, k = np.arange(P)[:, None], np.arange(3 * P)[None, :] - P
    mask = np.where(np.abs(q - k) <= P, 0.0, MASKED).astype(np.float32)
    return np.concatenate([np.concatenate([cos, cos]), np.concatenate([sin, -sin]), mask,
                           np.eye(P, dtype=np.float32)], axis=1)


def _stream(w_in, lru_wa, lru_wx, w_attn, w_rnn, w_out):
    def cols(w, at, n=P):
        return w[:, at:at + n].reshape(-1, P, n).transpose(1, 0, 2).reshape(P, -1)

    q0, k0, v0, ga0 = 0, 1024, 1280, 1536
    x0, gr0, ma0, mr0 = 2560, 3840, 5120, 6144
    def two(a, b):
        return [cols(w_in, a), cols(w_in, b)]

    def attn_branch(g):
        mine = w_attn[g * HEADS * P:(g + 1) * HEADS * P]
        return [cols(mine, d * P) for d in range(KT)]

    def rnn_branch(p, part):
        mine = w_rnn[2 * p * P:2 * (p + 1) * P]
        return [cols(mine, d * P) for d in range(part * KT // 2, (part + 1) * KT // 2)]

    def rnn_gates(b):
        return [lru_wa[0, b], lru_wa[1, b], lru_wx[0, b], lru_wx[1, b]]

    first_block = two(x0, gr0)
    out = two(k0, v0)
    for g in range(N_GROUPS):
        for h in range(g * HEADS, (g + 1) * HEADS):
            out += two(q0 + h * P, ga0 + h * P)
        out += two(k0 + (g + 1) * P, v0 + (g + 1) * P) if g < N_GROUPS - 1 else first_block
        out += attn_branch(g)
    out += rnn_gates(0) + two(x0 + P, gr0 + P) + rnn_gates(1)
    for p in range(1, PAIRS):
        for j in range(2):
            b = 2 * p + j
            out += two(x0 + b * P, gr0 + b * P) + rnn_gates(b) + rnn_branch(p - 1, j)
    out += two(ma0, mr0) + rnn_branch(PAIRS - 1, 0) + rnn_branch(PAIRS - 1, 1)
    w_out_units = [cols(w_out[2 * k * P:2 * (k + 1) * P], h * HALF, HALF) for h in range(2) for k in range(KT // 2)]
    for first_d, count, _, before in TILES_C:
        for d in range(first_d, first_d + count):
            out += two(ma0 + d * P, mr0 + d * P)
        out += w_out_units[before:before + 2] if before < 4 else w_out_units[4:]
    return np.concatenate(out, axis=1)


def _small(b_in, conv_w, conv_b, ba, bx, lam):
    b = b_in.reshape(56, P)
    q0, k0, v0, ga0, x0, gr0, ma0, mr0 = 0, 8, 10, 12, 20, 30, 40, 48
    order = []
    for g in range(N_GROUPS):
        order += [k0 + g, v0 + g]
        for h in range(g * HEADS, (g + 1) * HEADS):
            order += [q0 + h, ga0 + h]
    for n in range(RNN_BLOCKS):
        order += [x0 + n, gr0 + n]
    for d in range(KT):
        order += [ma0 + d, mr0 + d]
    rows = [b[order], conv_w.reshape(-1, P), conv_b.reshape(-1, P), ba.reshape(-1, P),
            bx.reshape(-1, P), lam.reshape(-1, P)]
    return np.ascontiguousarray(np.concatenate(rows, axis=0).T)


def kernel(x, w_in, b_in, attn_sink, conv_w, conv_b, lru_wa, lru_ba, lru_wx, lru_bx, lru_lambda,
           w_branch_attn, w_branch_rnn, w_out, b_out, ln_gain, ln_bias):
    import concourse.bacc as bacc
    from concourse.bass_utils import run_bass_kernel_spmd as run

    arrays = {
        "x_t": np.ascontiguousarray(np.asarray(x)[0].T.reshape(KT, P, SEQ).transpose(1, 0, 2)),
        "x_rows": np.ascontiguousarray(np.asarray(x)[0]),
        "stream": _stream(*(np.asarray(a)[0] for a in (w_in, lru_wa, lru_wx, w_branch_attn,
                                                       w_branch_rnn, w_out))),
        "small": _small(*(np.asarray(a)[0] for a in (b_in, conv_w, conv_b, lru_ba, lru_bx, lru_lambda))),
        "tables": _tables(),
        "sink": np.ascontiguousarray(np.asarray(attn_sink)[0]),
        "b_out": np.ascontiguousarray(np.asarray(b_out)[0]),
        "ln_gain": np.ascontiguousarray(np.asarray(ln_gain)[0]),
        "ln_bias": np.ascontiguousarray(np.asarray(ln_bias)[0]),
    }
    nc = bacc.Bacc("TRN2", target_bir_lowering=False, num_devices=1)
    args = [nc.dram_tensor(name, a.shape, mybir.dt.from_np(a.dtype), kind="ExternalInput").ap()
            for name, a in arrays.items()]
    args.append(nc.dram_tensor("out", (SEQ, D_MODEL), mybir.dt.float32, kind="ExternalOutput").ap())
    encoder_layer(nc, *args)
    r = run(nc, [arrays], core_ids=[0])
    return r.results[0]["out"].reshape(1, SEQ, D_MODEL)
```

```python
import numpy as np
import concourse.bass as bass
from concourse import mybir
from contextlib import ExitStack

P = 128
D_MODEL, SEQ = 1024, 1024
HEAD_DIM, N_HEADS, N_GROUPS = 128, 8, 2
HEADS = N_HEADS // N_GROUPS
D_RNN = 1280
RNN_BLOCKS = D_RNN // P
PAIRS = RNN_BLOCKS // 2
KT = D_MODEL // P
NB = SEQ // P
HALF = 512
UNIT = KT * P
EARLY = 3 * P
WARM_UP = 10
CONV_W, CONV_LEFT = 4, 2
SCALE = HEAD_DIM ** -0.5
ALPHA = 2.0 ** 0.25
LN_EPS = 1e-5
LRU_C = 8.0
ROPE_THETA = 10000.0
MASKED = -1.0e30

UNITS_GROUP = 2 * HEADS + 2 + 4
UNIT_B = 2 + N_GROUPS * UNITS_GROUP - 4
UNITS_FIRST = 8
UNITS_PAIR = 8
UNIT_P = UNIT_B + UNITS_FIRST
WIDTHS_FIRST = (HALF, UNIT, UNIT, UNIT, UNIT, HALF, UNIT, UNIT)
WIDTHS_PAIR = (UNIT, UNIT, HALF, UNIT) * 2
UNIT_C = UNIT_P + (PAIRS - 1) * UNITS_PAIR
TILES_C = ((1, 2, UNIT_C + 4, 0), (3, 2, UNIT_C + 10, 2), (5, 3, UNIT_C + 16, 4))
UNIT_WO0 = (UNIT_C + 8, UNIT_C + 14)
UNIT_WO1 = UNIT_C + 22
COLS_B = UNIT_B * UNIT
COLS_P = COLS_B + sum(WIDTHS_FIRST)
COLS_PAIR = sum(WIDTHS_PAIR)
COLS_C = COLS_P + (PAIRS - 1) * COLS_PAIR

FILLS_GROUP = HEADS + 1 + 4
FILL_X0 = N_GROUPS * FILLS_GROUP - 4
FILL_X1 = FILL_X0 + 3
FILL_P = FILL_X1 + 3
FILLS_PAIR = 6
FILL_C = FILL_P + (PAIRS - 1) * FILLS_PAIR
FILL_D = FILL_C + 5 + KT - 1

B_IN, CONV_WEIGHT, CONV_BIAS, GATE_A, GATE_X, LAMBDA = 0, 56, 96, 106, 126, 146
N_SMALL = 166
B_RNN = N_GROUPS * (2 + 2 * HEADS)
B_MERGE = B_RNN + 2 * RNN_BLOCKS
N_ROTARY, N_BANDS = 2 * SEQ, 4 * P


def encoder_layer(nc, x_t, x_rows, stream, small, tables, sink, b_out, ln_gain, ln_bias, out):
    f32, f32r = mybir.dt.float32, mybir.dt.float32r
    ALU, ACT = mybir.AluOpType, mybir.ActivationFunctionType
    ds = bass.ds
    ctx = ExitStack()
    with ctx:
        def allot(where, name, shape, dt=f32):
            return where.enter_context(nc.sbuf_tensor(name, shape, dt))

        raw = allot(ctx, "raw", [P, 2, UNIT])
        w_hi = allot(ctx, "w_hi", [P, 2, UNIT], f32r)
        w_lo = allot(ctx, "w_lo", [P, 2, UNIT], f32r)
        gates_hi = allot(ctx, "gates_hi", [P, HALF], f32r)
        gates_lo = allot(ctx, "gates_lo", [P, HALF], f32r)
        par = allot(ctx, "par", [P, N_SMALL])
        half_b = allot(ctx, "half_b", [P, B_RNN])
        rate = allot(ctx, "rate", [P, 2 * RNN_BLOCKS])
        nrate = allot(ctx, "nrate", [P, 2 * RNN_BLOCKS])
        nsink = allot(ctx, "nsink", [P, N_HEADS])
        nsink_now = allot(ctx, "nsink_now", [P, 1])
        neg_max = allot(ctx, "neg_max", [P, 1])
        denom = allot(ctx, "denom", [P, 1])
        rdenom = allot(ctx, "rdenom", [P, 1])
        stats = allot(ctx, "stats", [P, NB, 2, 6])
        moments = allot(ctx, "moments", [P, NB, 2])
        norm = allot(ctx, "norm", [P, NB, 4])
        norm_scratch = allot(ctx, "norm_scratch", [P, 3, 2 * RNN_BLOCKS])

        with ExitStack() as later:
            wo1_hi = allot(later, "wo1_hi", [P, KT, HALF], f32r)
            wo1_lo = allot(later, "wo1_lo", [P, KT, HALF], f32r)
            rows = allot(later, "rows", [P, NB, D_MODEL])
        xt_hi = allot(ctx, "xt_hi", [P, KT, SEQ], f32r)
        xt_lo = allot(ctx, "xt_lo", [P, KT, SEQ], f32r)

        with ExitStack() as stage:
            with ExitStack() as first:
                x_raw = allot(first, "x_raw", [P, KT, SEQ])
            at_hi = allot(stage, "at_hi", [P, HEADS * SEQ], f32r)
            at_lo = allot(stage, "at_lo", [P, HEADS * SEQ], f32r)
            k_hi = allot(stage, "k_hi", [P, SEQ], f32r)
            k_lo = allot(stage, "k_lo", [P, SEQ], f32r)
            v_hi = allot(stage, "v_hi", [P, SEQ], f32r)
            v_lo = allot(stage, "v_lo", [P, SEQ], f32r)
            q_hi = allot(stage, "q_hi", [P, SEQ], f32r)
            q_lo = allot(stage, "q_lo", [P, SEQ], f32r)
            pt_hi = allot(stage, "pt_hi", [P, 12, P], f32r)
            pt_lo = allot(stage, "pt_lo", [P, 12, P], f32r)
            gate = allot(stage, "gate", [P, SEQ])
            gated = allot(stage, "gated", [P, SEQ])
            tanh_g = allot(stage, "tanh_g", [P, SEQ])
            rot_a = allot(stage, "rot_a", [P, SEQ])
            rot_b = allot(stage, "rot_b", [P, SEQ])
            rotary = allot(stage, "rotary", [P, N_ROTARY])
            allot(stage, "spare", [P, CONV_W])
            bands = allot(stage, "bands", [P, N_BANDS])
            masked = allot(stage, "masked", [P, 3 * P + 1])
            probs = allot(stage, "probs", [P, 2, 3 * P + 1])
            part = allot(stage, "part", [P, 2, SEQ])
            cos, sin = rotary[:, 0:SEQ], rotary[:, SEQ:2 * SEQ]
            mask, ident = bands[:, 0:3 * P], bands[:, 3 * P:4 * P]
        with ExitStack() as stage:
            merged_hi = allot(stage, "merged_hi", [P, KT, SEQ], f32r)
            with ExitStack() as last:
                gain = allot(last, "gain", [P, D_MODEL])
                shift = allot(last, "shift", [P, D_MODEL])
                bias_o = allot(last, "bias_o", [P, D_MODEL])
            gate_a = allot(stage, "gate_a", [P, SEQ])
            gate_r = allot(stage, "gate_r", [P, SEQ])
            attn_in = allot(stage, "attn_in", [P, 2, SEQ])
            wo0_hi = allot(stage, "wo0_hi", [P, KT, HALF], f32r)
            wo0_lo = allot(stage, "wo0_lo", [P, KT, HALF], f32r)
            merged_lo = allot(stage, "merged_lo", [P, KT, SEQ], f32r)
        with ExitStack() as stage:
            racc = allot(stage, "racc", [P, KT, SEQ])
            decay = [allot(stage, f"decay{i}", [P, SEQ]) for i in range(2)]
            root = [allot(stage, f"root{i}", [P, SEQ]) for i in range(2)]
            state = [allot(stage, f"state{i}", [P, SEQ]) for i in range(2)]
            square = allot(stage, "square", [P, SEQ])
            h_hi, h_lo = [None, None], [None, None]
            h_hi[0] = allot(stage, "h_hi0", [P, 2, SEQ], f32r)
            h_lo[0] = allot(stage, "h_lo0", [P, 2, SEQ], f32r)
            silu_g = allot(stage, "silu_g", [P, SEQ])
            conv = allot(stage, "conv", [P, SEQ])
            conv_hi = allot(stage, "conv_hi", [P, SEQ], f32r)
            conv_lo = allot(stage, "conv_lo", [P, SEQ], f32r)
            padded = allot(stage, "padded", [P, SEQ + CONV_W])
            h_hi[1] = allot(stage, "h_hi1", [P, 2, SEQ], f32r)
            h_lo[1] = allot(stage, "h_lo1", [P, 2, SEQ], f32r)

        buf = [ctx.enter_context(nc.psum_tensor(f"proj{i}", [P, 2 * HALF], f32)) for i in range(2)]
        aux = [ctx.enter_context(nc.psum_tensor(f"aux{i}", [P, 2 * HALF], f32)) for i in range(2)]
        s_ps, pt_ps, ot_ps = aux[0][:, 0:HALF], aux[0][:, HALF:2 * HALF], aux[1]
        spill = nc.dram_tensor("spill", (N_GROUPS, P, KT * SEQ), f32, kind="Internal").ap()

        def sem(name):
            return ctx.enter_context(nc.semaphore(name))

        x_landed = [sem(f"x_landed{k}") for k in range(KT)]
        early_landed = sem("early_landed")
        early_hi_done = sem("early_hi_done")
        early_split = sem("early_split")
        v_zero = sem("v_zero")
        small_landed = sem("small_landed")
        table_landed = sem("table_landed")
        raw_landed = [sem(f"raw_landed{i}") for i in range(2)]
        unit_split = sem("unit_split")
        unit_begun = sem("unit_begun")
        racc_zero = sem("racc_zero")
        x_hi_done = sem("x_hi_done")
        x_split = sem("x_split")
        filled = [sem(f"filled{i}") for i in range(2)]
        freed = [sem(f"freed{i}") for i in range(2)]
        consts_act = sem("consts_act")
        dve_chain = sem("dve_chain")
        act_chain = sem("act_chain")
        roped = sem("roped")
        roped_hi = sem("roped_hi")
        roped_split = sem("roped_split")
        v_turned = sem("v_turned")
        v_hi_done = sem("v_hi_done")
        v_split = sem("v_split")
        silu_done = sem("silu_done")
        scores_done = sem("scores_done")
        scores_masked = sem("scores_masked")
        exp_done = sem("exp_done")
        probs_ready = sem("probs_ready")
        pt_done = sem("pt_done")
        pt_hi_done = sem("pt_hi_done")
        pt_split = sem("pt_split")
        pv_done = sem("pv_done")
        attn_gated = sem("attn_gated")
        attn_hi_done = sem("attn_hi_done")
        attn_split = sem("attn_split")
        spilled = [sem(f"spilled{i}") for i in range(2)]
        padding_zero = sem("padding_zero")
        conv_begun = sem("conv_begun")
        convolved = sem("convolved")
        conv_hi_done = sem("conv_hi_done")
        conv_split = sem("conv_split")
        conv_used = sem("conv_used")
        sigm_g_done = sem("sigm_g_done")
        gate_filled = [sem(f"gate_filled{i}") for i in range(2)]
        gate_freed = [sem(f"gate_freed{i}") for i in range(2)]
        squared = sem("squared")
        one_less = sem("one_less")
        rooted = sem("rooted")
        rnn_done = sem("rnn_done")
        rnn_hi_done = sem("rnn_hi_done")
        rnn_split = sem("rnn_split")
        attn_in_landed = sem("attn_in_landed")
        attn_in_used = sem("attn_in_used")
        merged_done = sem("merged_done")
        merged_hi_done = sem("merged_hi_done")
        merged_split = sem("merged_split")
        rows_landed = sem("rows_landed")
        ln_landed = sem("ln_landed")
        out_done = sem("out_done")
        out_added = sem("out_added")
        var_done = sem("var_done")
        root_done = sem("root_done")
        scaled_by = sem("scaled_by")
        normed = sem("normed")
        gained = sem("gained")
        shifted = sem("shifted")
        last_shifted = sem("last_shifted")
        stored = sem("stored")
        pool_waited = sem("pool_waited")
        dve_waited = sem("dve_waited")
        pool_chain = sem("pool_chain")
        act_tanh = sem("act_tanh")
        act_decay = sem("act_decay")
        sink_placed = sem("sink_placed")
        rdenom_done = sem("rdenom_done")
        tap_done = sem("tap_done")
        u_done = sem("u_done")
        scanned = sem("scanned")
        mixed = sem("mixed")
        resid = sem("resid")
        stats_done = sem("stats_done")

        def bias(col):
            return par[:, ds(B_IN + col, 1)]

        def key_blocks(n):
            return list(range(max(n - 1, 0), min(n + 1, NB - 1) + 1))

        def pt_segments(n):
            runs = []
            for i, kb in enumerate(key_blocks(n)):
                slot = 3 * (kb % 4) + n - kb + 1
                if runs and slot == runs[-1][2] + 2 * runs[-1][1]:
                    runs[-1][1] += 1
                else:
                    runs.append([i, 1, slot])
            return runs

        NEXT_SCORES = 1
        SLICES = {1: 2, 2: 2, 3: 1, 4: 2, 5: 1, 6: 2, 7: 1, 8: 2, 9: 1, 10: 2}
        row_bank = [t[:, h * HALF:(h + 1) * HALF] for t in aux + buf for h in range(2)]

        halves = [slice(0, HALF), slice(HALF, D_MODEL)]

        block = ctx.enter_context(nc.Block())

        @block.sync
        def _(sp):
            def load(index, slot, col, cols=UNIT):
                sp.wait_ge(unit_split, index + 1)
                sp.dma_start(raw[:, slot, 0:cols], stream[:, ds(col, cols)]).then_inc(raw_landed[slot], 16)

            sp.dma_start(raw[:, 0, 0:EARLY], stream[:, 0:EARLY]).then_inc(early_landed, 16)
            for k in range(KT):
                sp.dma_start(x_raw[:, k, :], x_t[:, k, :]).then_inc(x_landed[k], 16)
                if k == 1:
                    sp.dma_start(raw[:, 0, EARLY:UNIT], stream[:, EARLY:UNIT]).then_inc(raw_landed[0], 16)
                if k == 5:
                    load(1, 1, UNIT)
            sp.dma_start(rotary[:, :], tables[:, 0:N_ROTARY]).then_inc(table_landed, 16)
            sp.dma_start(bands[:, :], tables[:, N_ROTARY:]).then_inc(table_landed, 16)
            with sp.Fori(1, UNIT_B // 2) as i:
                for n in range(2):
                    load(i * 2 + n, n, i * (2 * UNIT) + n * UNIT)
            at = COLS_B
            for n, cols in enumerate(WIDTHS_FIRST):
                load(UNIT_B + n, n % 2, at, cols)
                at += cols
            with sp.Fori(0, PAIRS - 1) as p:
                at = COLS_P
                for n, cols in enumerate(WIDTHS_PAIR):
                    load(p * UNITS_PAIR + UNIT_P + n, n % 2, p * COLS_PAIR + at, cols)
                    at += cols
            for n in range(2):
                load(UNIT_C + n, n, COLS_C + n * UNIT)
            for i in range(2):
                sp.wait_ge(spilled[i], 16 * (1 + 4 * N_GROUPS))
            sp.wait_ge(u_done, 2 * RNN_BLOCKS)

            def load_attn(d):
                sp.wait_ge(attn_in_used, d + 1)
                sp.dma_start(attn_in[:, :, :], spill[:, :, ds(d * SEQ, SEQ)]
                             .rearrange("g p s -> p g s")).then_inc(attn_in_landed, 16)

            load_attn(0)
            for n in range(2):
                load(UNIT_C + 2 + n, n, COLS_C + (2 + n) * UNIT)
            for first_d, count, unit, before in TILES_C:
                with sp.Fori(0, count) as i:
                    for n in range(2):
                        load(i * 2 + unit + n, n, i * (2 * UNIT) + COLS_C + (unit - UNIT_C + n) * UNIT)
                    load_attn(i + first_d)
                if before < 4:
                    for n in range(2):
                        wo0 = UNIT_WO0[before // 2] + n
                        load(wo0, n, COLS_C + (wo0 - UNIT_C) * UNIT)
            for n in range(4):
                load(UNIT_WO1 + n, n % 2, COLS_C + (UNIT_WO1 - UNIT_C + n) * UNIT)
            sp.wait_ge(filled[0], FILL_D)
            sp.wait_ge(filled[1], FILL_D)
            for n in range(NB):
                sp.dma_start(rows[:, n, :], x_rows[n * P:(n + 1) * P, :]).then_inc(rows_landed, 16)
            sp.wait_ge(merged_split, KT + 1)
            for dst, src in ((bias_o, b_out), (gain, ln_gain), (shift, ln_bias)):
                sp.dma_start(dst[:, :], src.partition_broadcast(P)).then_inc(ln_landed, 16)
            for n in range(NB - 1):
                sp.wait_ge(shifted, n + 1)
                sp.dma_start(out[n * P:(n + 1) * P, :], rows[:, n, :]).then_inc(stored, 16)
            for i, c in enumerate(halves):
                sp.wait_ge(last_shifted, i + 1)
                sp.dma_start(out[(NB - 1) * P:NB * P, c], rows[:, NB - 1, c]).then_inc(stored, 16)
            sp.wait_ge(stored, 16 * (NB + 1))

        @block.gpsimd
        def _(pool):
            pool.sem_inc(unit_split, 2)

            def split(index, raw_slot, cols, hi, lo):
                pool.wait_ge(raw_landed[raw_slot], (index - raw_slot) * 8 + 16)
                pool.sem_inc(pool_waited, 1)
                nc.gpsimd.tensor_scalar(hi, raw[:, raw_slot, cols], 1.0, 0.0, ALU.mult, ALU.add)\
                    .then_inc(pool_chain, 1)
                pool.wait_ge(pool_chain, index + 1)
                nc.gpsimd.tensor_tensor(lo, raw[:, raw_slot, cols], hi.bitcast(f32), ALU.subtract)\
                    .then_inc(unit_split, 1)

            def ring(index, number, raw_slot, slot):
                pool.wait_ge(unit_begun, number + 1)
                split(index, raw_slot, slice(0, UNIT), w_hi[:, slot, :], w_lo[:, slot, :])

            def gate_weights(index, raw_slot, b):
                if b is not None:
                    pool.wait_ge(gate_filled[1], b * 2)
                split(index, raw_slot, slice(0, HALF), gates_hi[:, :], gates_lo[:, :])

            def output_weights(unit, count, hi, lo, k):
                for n in range(count):
                    two = slice(k + 2 * n, k + 2 * n + 2)
                    split(unit + n, n % 2, slice(0, UNIT), hi[:, two, :].rearrange("p k c -> p (k c)"),
                          lo[:, two, :].rearrange("p k c -> p (k c)"))

            pool.wait_ge(early_landed, 16)
            nc.gpsimd.tensor_scalar(w_hi[:, 0, 0:EARLY], raw[:, 0, 0:EARLY], 1.0, 0.0, ALU.mult, ALU.add)\
                .then_inc(early_hi_done, 1)
            pool.wait_ge(early_hi_done, 1)
            nc.gpsimd.tensor_tensor(w_lo[:, 0, 0:EARLY], raw[:, 0, 0:EARLY],
                                    w_hi[:, 0, 0:EARLY].bitcast(f32), ALU.subtract).then_inc(early_split, 1)
            split(0, 0, slice(EARLY, UNIT), w_hi[:, 0, EARLY:UNIT], w_lo[:, 0, EARLY:UNIT])
            ring(1, 1, 1, 1)
            with pool.Fori(1, UNIT_B // 2) as i:
                for n in range(2):
                    ring(i * 2 + n, i * 2 + n, n, n)
            gate_weights(UNIT_B, 0, None)
            for n in range(1, 5):
                ring(UNIT_B + n, UNIT_B + n - 1, n % 2, (n - 1) % 2)
            gate_weights(UNIT_B + 5, 1, 1)
            for n in range(6, UNITS_FIRST + 2):
                ring(UNIT_B + n, UNIT_B + n - 2, n % 2, n % 2)
            for b in range(2):
                pool.wait_ge(filled[b], FILL_P)
            nc.gpsimd.memset(racc[:, :, :], 0.0).then_inc(racc_zero, 1)
            with pool.Fori(0, PAIRS - 1) as p:
                for j in range(2):
                    unit = p * UNITS_PAIR + UNIT_P + 4 * j + 2
                    gate_weights(unit, 0, p * 2 + 2 + j)
                    for n in range(1, 4):
                        number = p * (UNITS_PAIR - 2) + (UNIT_P - 2 + 3 * j + 1 + n)
                        ring(unit + n, number, n % 2, (j + n + 1) % 2)
            for n in range(2, 4):
                ring(UNIT_C + n, UNIT_C + n - RNN_BLOCKS, n % 2, n % 2)
            for first_d, count, unit, before in TILES_C:
                with pool.Fori(0, count) as i:
                    for n in range(2):
                        ring(i * 2 + unit + n, i * 2 + (unit + n - RNN_BLOCKS - before), n, n)
                if before < 4:
                    if before == 0:
                        pool.wait_ge(rnn_split, RNN_BLOCKS + 1)
                    output_weights(UNIT_WO0[before // 2], 2, wo0_hi, wo0_lo, 2 * before)
            pool.wait_ge(filled[0], FILL_D)
            pool.wait_ge(filled[1], FILL_D)
            output_weights(UNIT_WO1, 4, wo1_hi, wo1_lo, 0)
            pool.wait_ge(ln_landed, 48)
            for n in range(NB - 1):
                pool.wait_ge(gained, n + 1)
                nc.gpsimd.tensor_tensor(rows[:, n, :], rows[:, n, :], shift[:, :], ALU.add)\
                    .then_inc(shifted, 1)

        @block.tensor
        def _(pe):
            pe.sem_inc(unit_begun, 1)
            pe.sem_inc(scores_done, 1)
            pe.sem_inc(pt_done, 2)
            pe.sem_inc(pv_done, NB)

            def part_slice(slot, col, banks, mov_hi, mov_lo, first, last):
                return products(w_hi[:, slot, col:col + P], w_lo[:, slot, col:col + P], banks,
                                mov_hi, mov_lo, first, last)

            def products(wh, wl, banks, mov_hi, mov_lo, first, last):
                begun = None
                for h in range(2):
                    i = nc.tensor.matmul(banks[:, h * HALF:(h + 1) * HALF], wh,
                                         mov_hi[:, h * HALF:(h + 1) * HALF], start=first, stop=False)
                    begun = begun or i
                    nc.tensor.matmul(banks[:, h * HALF:(h + 1) * HALF], wh,
                                     mov_lo[:, h * HALF:(h + 1) * HALF], start=False, stop=False)
                for h in range(2):
                    i = nc.tensor.matmul(banks[:, h * HALF:(h + 1) * HALF], wl,
                                         mov_hi[:, h * HALF:(h + 1) * HALF], start=False, stop=last)
                return begun, i

            def tile_slice(k, unit, slot, fill, b):
                if k == 0:
                    pe.wait_ge(unit_split, unit + 3)
                    pe.wait_ge(freed[b], fill + 1)
                first, last = part_slice(slot, k * P, buf[b], xt_hi[:, k, :], xt_lo[:, k, :],
                                         k == 0, k == KT - 1)
                if k == 0:
                    first.then_inc(unit_begun, 1)
                if k == KT - 1:
                    last.then_inc(filled[b], 1)

            def tile(unit, slot, fill, b):
                for k in range(KT):
                    tile_slice(k, unit, slot, fill, b)

            def scores(m, n):
                pe.wait_ge(scores_masked, m + n + 1)
                ks = key_blocks(n)
                q = slice(n * P, (n + 1) * P)
                keys = slice(ks[0] * P, (ks[-1] + 1) * P)
                dst = s_ps[:, 0:len(ks) * P]
                nc.tensor.matmul(dst, q_hi[:, q], k_hi[:, keys], start=True, stop=False)
                nc.tensor.matmul(dst, q_hi[:, q], k_lo[:, keys], start=False, stop=False)
                nc.tensor.matmul(dst, q_lo[:, q], k_hi[:, keys], start=False, stop=True)\
                    .then_inc(scores_done, 1)

            def transpose_probs(m, n):
                pe.wait_ge(probs_ready, m + n + 2)
                pe.wait_ge(pt_split, m + n + 1)
                nk = len(key_blocks(n))
                for i in range(nk):
                    at = (3 - nk + i) * P
                    last = nc.tensor.transpose(pt_ps[:, i * P:(i + 1) * P], probs[:, n % 2, at:at + P],
                                               ident)
                last.then_inc(pt_done, 1)

            def weigh_values(head2, m, kb):
                pe.wait_ge(pt_split, m + min(kb + 1, NB - 1) + 2)
                if kb == 0:
                    pe.wait_ge(attn_gated, head2 + 1)
                if kb == NB // 2 - 1:
                    pe.wait_ge(attn_gated, head2 + 2)
                lo, hi = max(kb - 1, 0), min(kb + 1, NB - 1)
                half = NB // 2
                runs = [(a, z) for a, z in ((lo, min(hi, half - 1)), (max(lo, half), hi)) if a <= z]
                for v, p in ((v_hi, pt_hi), (v_hi, pt_lo), (v_lo, pt_hi)):
                    for a, z in runs:
                        slot = 3 * (kb % 4) + a - kb + 1
                        opens = v is v_hi and p is pt_hi and (a, kb) in ((0, 0), (half, half - 1))
                        last = nc.tensor.matmul(
                            ot_ps[:, a * P:(z + 1) * P], v[:, kb * P:(kb + 1) * P],
                            p[:, slot:slot + z - a + 1, :].rearrange("p n c -> p (n c)"),
                            start=opens, stop=v is v_lo, skip_group_check=True)
                last.then_inc(pv_done, 1)

            def attention(g, h, unit, fill, more):
                m = h * NB + g * HEADS * NB
                at = 0
                for n in range(1, NB + 3):
                    if n < NB:
                        scores(m, n)
                    if n == NB + 2:
                        weigh_values(h * 2 + g * 2 * HEADS, m, NB - 1)
                    share = SLICES[n]
                    for i in range(share):
                        if i == share // 2 and n <= NB:
                            transpose_probs(m, n - 1)
                        if i == NEXT_SCORES and n == NB + 2 and more:
                            pe.wait_ge(roped_split, h + g * (HEADS + 1) + 4)
                            scores(m + NB, 0)
                        b, k = divmod(at, KT)
                        tile_slice(k, unit + b, b, fill, b)
                        at += 1
                    if 3 <= n < NB + 2:
                        if n == 3:
                            pe.wait_ge(v_split, g + 1)
                        weigh_values(h * 2 + g * 2 * HEADS, m, n - 3)

            def attention_branch(g, unit, slot, fill, b):
                pe.wait_ge(unit_split, unit + 3)
                pe.wait_ge(freed[b], fill + 1)
                for k in range(HEADS):
                    pe.wait_ge(attn_split, (g * HEADS + k + 1) * 2 + 2)
                    first, last = part_slice(slot, (b * HEADS + k) * P, buf[b],
                                             at_hi[:, k * SEQ:(k + 1) * SEQ],
                                             at_lo[:, k * SEQ:(k + 1) * SEQ], k == 0, k == HEADS - 1)
                    if b == 0 and k == 0:
                        first.then_inc(unit_begun, 1)
                last.then_inc(filled[b], 1)

            pe.wait_ge(v_zero, 1)
            for _ in range(WARM_UP):
                nc.tensor.matmul(aux[0][:, 0:HALF], v_lo[:, 0:P], v_lo[:, 0:HALF], start=True, stop=True)
            pe.wait_ge(freed[0], 1)
            for k in range(KT):
                if k in (0, EARLY // P):
                    pe.wait_ge(*((unit_split, 3) if k else (early_split, 1)))
                pe.wait_ge(x_split, k + 1)
                first, last = part_slice(0, k * P, buf[0], xt_hi[:, k, :], xt_lo[:, k, :],
                                         k == 0, k == KT - 1)
                if k == 0:
                    first.then_inc(unit_begun, 1)
            last.then_inc(filled[0], 1)
            tile(1, 1, 0, 1)
            for g in range(N_GROUPS):
                unit, fill = 2 + g * UNITS_GROUP, 1 + g * FILLS_GROUP
                tile(unit, 0, fill, 0)
                pe.wait_ge(freed[1], fill + 1)
                pe.wait_ge(table_landed, 32)
                pe.wait_ge(attn_gated, g * 2 * HEADS + 2)
                for n in range(NB):
                    last = nc.tensor.transpose(ot_ps[:, n * P:(n + 1) * P], tanh_g[:, n * P:(n + 1) * P],
                                               ident)
                last.then_inc(v_turned, 1)
                for k in range(KT):
                    if k == KT - 1:
                        pe.wait_ge(roped_split, g * (HEADS + 1) + 3)
                        scores(g * HEADS * NB, 0)
                    tile_slice(k, unit + 1, 1, fill, 1)
                with pe.Fori(0, HEADS - 1) as h:
                    attention(g, h, h * 2 + (unit + 2), h + (fill + 1), True)
                attention(g, HEADS - 1, unit + 2 * HEADS, fill + HEADS, False)
                if g < N_GROUPS - 1:
                    for n in range(KT // 2):
                        for b in range(2):
                            attention_branch(g, unit + 2 * HEADS + 2 + n, n % 2, fill + HEADS + 1 + n, b)

            def gates(unit, b_index, n):
                if n == 0:
                    pe.wait_ge(unit_split, unit + 3)
                    pe.wait_ge(conv_split, b_index + 1)
                for d in range(2):
                    c = slice((2 * n + d) * P, (2 * n + d + 1) * P)
                    pe.wait_ge(gate_freed[d], b_index * 2 + n + 1)
                    _, last = products(gates_hi[:, c], gates_lo[:, c], aux[d], conv_hi, conv_lo, True, True)
                    last.then_inc(gate_filled[d], 1)

            def rnn_branch(unit, slot, fill, pair, tiles):
                if tiles[0] == 0:
                    pe.wait_ge(unit_split, unit + 3)
                for j in tiles:
                    b = j % 2
                    pe.wait_ge(freed[b], fill + j // 2 + 1)
                    for k in range(2):
                        first, last = part_slice(slot, (2 * j + k) * P, buf[b], h_hi[pair][:, k, :],
                                                 h_lo[pair][:, k, :], k == 0, k == 1)
                        if j == 0 and k == 0:
                            first.then_inc(unit_begun, 1)
                    last.then_inc(filled[b], 1)

            def first_gates(unit, slot, b_index, fill):
                g = N_GROUPS - 1
                gates(unit, b_index, 0)
                attention_branch(g, unit + 1, slot, fill, 0)
                gates(unit, b_index, 1)
                attention_branch(g, unit + 1, slot, fill, 1)
                for b in range(2):
                    attention_branch(g, unit + 2, 1 - slot, fill + 1, b)

            pe.wait_ge(scores_masked, N_HEADS * NB + 1)
            pe.wait_ge(pt_split, N_HEADS * NB + 1)
            pe.wait_ge(attn_gated, 2 * N_HEADS + 2)
            first_gates(UNIT_B, 0, 0, FILL_X0 + 1)
            tile(UNIT_B + 3, 0, FILL_X1, 0)
            tile(UNIT_B + 4, 1, FILL_X1, 1)
            first_gates(UNIT_B + 5, 0, 1, FILL_X1 + 1)
            with pe.Fori(0, (PAIRS - 1) // 2) as pp:
                for i in range(2):
                    for j in range(2):
                        u = pp * (2 * UNITS_PAIR) + UNIT_P + i * UNITS_PAIR + 4 * j
                        f = pp * (2 * FILLS_PAIR) + FILL_P + i * FILLS_PAIR + 3 * j
                        b_index = pp * 4 + 2 + 2 * i + j
                        tile(u, j, f, 0)
                        tile(u + 1, 1 - j, f, 1)
                        gates(u + 2, b_index, 0)
                        if j == 0:
                            pe.wait_ge(rnn_split, b_index + 1)
                        rnn_branch(u + 3, j, f + 1, i, (0,))
                        gates(u + 2, b_index, 1)
                        rnn_branch(u + 3, j, f + 1, i, (1, 2, 3))

            tile(UNIT_C, 0, FILL_C, 0)
            tile(UNIT_C + 1, 1, FILL_C, 1)
            pe.wait_ge(rnn_split, RNN_BLOCKS + 1)
            for n in range(2):
                rnn_branch(UNIT_C + 2 + n, n, FILL_C + 1 + 2 * n, (PAIRS - 1) % 2, range(4))
            for first_d, count, unit, before in TILES_C:
                with pe.Fori(0, count) as i:
                    tile(i * 2 + unit, 0, i + (FILL_C + 4 + first_d), 0)
                    tile(i * 2 + unit + 1, 1, i + (FILL_C + 4 + first_d), 1)

            def rows_slice(n, half, k):
                wh, wl = ((wo0_hi, wo0_lo), (wo1_hi, wo1_lo))[half]
                s = slice(n * P, (n + 1) * P)
                nc.tensor.matmul(row_bank[n], merged_hi[:, k, s], wh[:, k, :], start=k == 0, stop=False)
                nc.tensor.matmul(row_bank[n], merged_hi[:, k, s], wl[:, k, :], start=False, stop=False)
                last = nc.tensor.matmul(row_bank[n], merged_lo[:, k, s], wh[:, k, :],
                                        start=False, stop=k == KT - 1)
                if k == KT - 1:
                    last.then_inc(out_done, 1)

            pe.wait_ge(gate_freed[0], 2 * RNN_BLOCKS + 1)
            pe.wait_ge(gate_freed[1], 2 * RNN_BLOCKS + 1)
            pe.wait_ge(unit_split, UNIT_WO0[1] + 2 + 2)
            pe.wait_ge(merged_split, KT)
            for n in range(NB // 2):
                for k in range(KT - 1):
                    rows_slice(n, 0, k)
            pe.wait_ge(merged_split, KT + 1)
            for n in range(NB // 2):
                rows_slice(n, 0, KT - 1)
            pe.wait_ge(freed[0], FILL_D + 1)
            pe.wait_ge(freed[1], FILL_D + 1)
            for n in range(NB // 2, NB):
                for k in range(KT):
                    rows_slice(n, 0, k)
            pe.wait_ge(unit_split, UNIT_WO1 + 4 + 2)
            for n in range(NB):
                pe.wait_ge(out_added, n + 1)
                for k in range(KT):
                    rows_slice(n, 1, k)

        @block.scalar
        def _(act):
            for s, credit in ((exp_done, 1), (gate_freed[0], 1), (gate_freed[1], 1),
                              (spilled[0], 16), (spilled[1], 16), (freed[1], 1)):
                act.sem_inc(s, credit)
            act.dma_start(par[:, :], small).then_inc(small_landed, 16)
            act.dma_start(nsink[:, :], sink.partition_broadcast(P)).then_inc(small_landed, 16)
            act.wait_ge(v_zero, 1)
            nc.scalar.activation(v_hi[:, 0:1], v_lo[:, 0:1].bitcast(f32), ACT.Copy)

            def copy(dst, src):
                return nc.scalar.activation(dst, src, ACT.Copy)

            for k in range(KT):
                act.wait_ge(x_landed[k], 16)
                copy(xt_hi[:, k, :], x_raw[:, k, :]).then_inc(x_hi_done, 1)
            act.wait_ge(small_landed, 32)
            nc.scalar.activation(half_b[:, :], par[:, B_IN:B_IN + B_RNN], ACT.Copy, scale=0.5)\
                .then_inc(act_chain, 1)
            nc.scalar.activation(nrate[:, :], par[:, LAMBDA:LAMBDA + 2 * RNN_BLOCKS], ACT.Abs)\
                .then_inc(act_chain, 1)
            act.wait_ge(act_chain, 2)
            nc.scalar.activation(nrate[:, :], nrate[:, :], ACT.Exp, scale=-1.0).then_inc(consts_act, 1)

            def v_evac(g, fill, col):
                act.wait_ge(filled[1], fill + 1)
                act.wait_ge(silu_done, g * HEADS + 1)
                nc.scalar.activation(tanh_g[:, :], buf[1][:, :], ACT.Identity, bias=bias(col))\
                    .then_inc(freed[1], 1)

            def gate_evac(g, h):
                col = h * 2 + (g * (2 + 2 * HEADS) + 3)
                act.wait_ge(filled[1], h + (g * FILLS_GROUP + 2))
                act.wait_ge(attn_gated, h * 2 + (g * 2 * HEADS + 2))
                act.wait_ge(silu_done, h + (g * HEADS + 1))
                nc.scalar.activation(gate[:, :], buf[1][:, :], ACT.Identity, scale=0.5,
                                     bias=half_b[:, ds(col, 1)])
                nc.scalar.activation(tanh_g[:, :], buf[1][:, :], ACT.Tanh, scale=0.5,
                                     bias=half_b[:, ds(col, 1)]).then_inc(freed[1], 1)

            def rope_hi(dst, count, last_scores):
                act.wait_ge(roped, count)
                act.wait_ge(scores_done, last_scores + 1)
                copy(dst[:, :], rot_a[:, :]).then_inc(roped_hi, 1)

            def exponentials(m, n):
                c0 = (3 - len(key_blocks(n))) * P
                act.wait_ge(pt_done, m + n + 1)
                act.wait_ge(scores_masked, m + n + 2)
                nc.scalar.activation(probs[:, n % 2, c0:3 * P + 1], masked[:, c0:3 * P + 1],
                                     ACT.Exp, scale=-1.0, bias=neg_max[:, 0:1],
                                     accum_out=denom[:, 0:1]).then_inc(exp_done, 1)

            def attention_hi(g, h, half):
                act.wait_ge(attn_gated, h * 2 + (g * 2 * HEADS + half + 3))
                copy(at_hi[:, ds(h * SEQ + half * HALF, HALF)], gated[:, half * HALF:(half + 1) * HALF])\
                    .then_inc(attn_hi_done, 1)

            def attention(g, h, next_rope, more):
                first_conv = next_rope is None
                m = h * NB + g * HEADS * NB
                for n in range(1, NB + 3):
                    if n < NB:
                        exponentials(m, n)
                    if n <= NB:
                        q = n - 1
                        act.wait_ge(pv_done, m + min(q, NB - 2) + 6)
                        act.wait_ge(pt_done, m + q + 3)
                        for i, count, slot in pt_segments(q):
                            last = copy(pt_hi[:, slot:slot + 2 * count - 1:2, :],
                                        pt_ps[:, i * P:(i + count) * P].rearrange("p (n c) -> p n c", c=P))
                        last.then_inc(pt_hi_done, 1)
                    if n == 1:
                        gate_evac(g, h)
                    if n == NB - 2 and first_conv:
                        pad_x(0, FILL_X0)
                    if n == NB - 1 and first_conv:
                        act.wait_ge(roped_split, N_GROUPS * (HEADS + 1) + 1)
                        conv_begin(0, FILL_X0)
                    if n == NB + 1:
                        if next_rope is not None:
                            rope_hi(next_rope, h + (g * (HEADS + 1) + 3), m + NB)
                        attention_hi(g, h, 0)
                        if first_conv:
                            conv_high(0)
                    if n == NB + 2 and more:
                        exponentials(m + NB, 0)
                attention_hi(g, h, 1)

            def pad_x(b, fill):
                act.wait_ge(padding_zero, 2)
                act.wait_ge(convolved, b + 1)
                act.wait_ge(filled[0], fill + 1)
                nc.scalar.activation(padded[:, CONV_LEFT:CONV_LEFT + SEQ], buf[0][:, :], ACT.Identity,
                                     bias=bias(b * 2 + B_RNN)).then_inc(freed[0], 1)

            def conv_begin(b, fill):
                act.wait_ge(freed[0], fill + 2)
                act.wait_ge(conv_used, b + 1)
                nc.scalar.activation(conv[:, :], padded[:, 0:SEQ], ACT.Identity,
                                     scale=par[:, ds(b + CONV_WEIGHT, 1)],
                                     bias=par[:, ds(b + CONV_BIAS, 1)]).then_inc(conv_begun, 1)

            def conv_high(b):
                act.wait_ge(convolved, b + 2)
                copy(conv_hi[:, :], conv[:, :]).then_inc(conv_hi_done, 1)

            def silu_gate(b, fill):
                act.wait_ge(rnn_split, b + 1)
                act.wait_ge(filled[1], fill + 1)
                nc.scalar.activation(silu_g[:, :], buf[1][:, :], ACT.Sigmoid,
                                     bias=bias(b * 2 + B_RNN + 1)).then_inc(sigm_g_done, 1)

            def spill_branch(g, n, b, fill):
                act.wait_ge(spilled[b], g * (16 * KT // 2) + 16 * (n + 1))
                act.wait_ge(filled[b], fill + 1)
                copy(part[:, b, :], buf[b][:, :]).then_inc(freed[b], 1)
                act.wait_ge(freed[b], fill + 2)
                act.dma_start(spill[g, :, (2 * n + b) * SEQ:(2 * n + b + 1) * SEQ], part[:, b, :])\
                    .then_inc(spilled[b], 16)

            def recurrence(b, spill_tile):
                for n, (dst, first) in enumerate(((decay, GATE_A), (state, GATE_X))):
                    for d in range(2):
                        act.wait_ge(gate_filled[d], b * 2 + n + 1)
                        nc.scalar.activation(dst[d][:, :], aux[d][:, :], ACT.Sigmoid,
                                             bias=par[:, ds(b + first + d * RNN_BLOCKS, 1)])\
                            .then_inc(gate_freed[d], 1)
                    if n == 0:
                        spill_tile(0)
                for d in range(2):
                    act.wait_ge(gate_freed[d], b * 2 + 2)
                    nc.scalar.activation(root[d][:, :], decay[d][:, :], ACT.Tanh,
                                         scale=rate[:, ds(b + d * RNN_BLOCKS, 1)]).then_inc(act_tanh, 1)
                act.wait_ge(act_tanh, b * 2 + 2)
                for d in range(2):
                    nc.scalar.activation(decay[d][:, :], decay[d][:, :], ACT.Exp,
                                         scale=nrate[:, ds(b + d * RNN_BLOCKS, 1)]).then_inc(act_decay, 1)
                spill_tile(1)
                for d in range(2):
                    act.wait_ge(act_decay, b * 2 + d + 1)
                    if d == 1:
                        act.wait_ge(one_less, b * 2 + 1)
                    nc.scalar.activation(square[:, :], decay[d][:, :], ACT.Square).then_inc(squared, 1)
                spill_tile(2)
                for d in range(2):
                    act.wait_ge(one_less, b * 2 + d + 1)
                    nc.scalar.activation(root[d][:, :], root[d][:, :], ACT.Sqrt).then_inc(rooted, 1)
                spill_tile(3)

            def finish_block(b, pair, j):
                act.wait_ge(rnn_done, b + 1)
                copy(h_hi[pair][:, j, :], state[0][:, :]).then_inc(rnn_hi_done, 1)

            rope_hi(k_hi, 1, 0)
            v_evac(0, 0, 1)
            for g in range(N_GROUPS):
                rope_hi(q_hi, g * (HEADS + 1) + 2, g * HEADS * NB)
                act.wait_ge(v_turned, g + 1)
                act.wait_ge(pv_done, g * HEADS * NB + NB)
                copy(v_hi[:, :], ot_ps[:, :]).then_inc(v_hi_done, 1)
                exponentials(g * HEADS * NB, 0)
                with act.Fori(0, HEADS - 1) as h:
                    attention(g, h, q_hi, True)
                attention(g, HEADS - 1, k_hi if g < N_GROUPS - 1 else None, False)
                if g < N_GROUPS - 1:
                    v_evac(g + 1, g * FILLS_GROUP + HEADS + 1, (g + 1) * (2 + 2 * HEADS) + 1)
                    for n in range(KT // 2):
                        for b in range(2):
                            spill_branch(g, n, b, g * FILLS_GROUP + HEADS + 2 + n)

            silu_gate(0, FILL_X0)
            act.wait_ge(attn_split, 2 * N_HEADS + 2)
            last_g = N_GROUPS - 1
            recurrence(0, lambda n: spill_branch(last_g, n // 2, n % 2, FILL_X0 + 1 + n // 2))
            pad_x(1, FILL_X1)
            conv_begin(1, FILL_X1)
            finish_block(0, 0, 0)
            conv_high(1)
            silu_gate(1, FILL_X1)
            recurrence(1, lambda n: spill_branch(last_g, 2 + n // 2, n % 2, FILL_X1 + 1 + n // 2))
            for i in range(2):
                act.wait_ge(spilled[i], 16 * (1 + 4 * N_GROUPS))
            with act.Fori(0, (PAIRS - 1) // 2) as pp:
                for i in range(2):
                    for j in range(2):
                        b = pp * 4 + 2 + 2 * i + j
                        f = pp * (2 * FILLS_PAIR) + FILL_P + i * FILLS_PAIR + 3 * j
                        pad_x(b, f)
                        conv_begin(b, f)
                        finish_block(b - 1, 1 - i if j else i, 1 - j)
                        conv_high(b)
                        silu_gate(b, f)
                        recurrence(b, lambda n: None)
            finish_block(RNN_BLOCKS - 1, (PAIRS - 1) % 2, 1)

            def merge(d, fill):
                act.wait_ge(merged_split, d + 1)
                for b, dst in enumerate((gate_a, gate_r)):
                    act.wait_ge(filled[b], fill + 1)
                    nc.scalar.activation(dst[:, :], buf[b][:, :], ACT.Sigmoid,
                                         bias=bias(d * 2 + B_MERGE + b)).then_inc(freed[b], 1)
                act.wait_ge(merged_done, d + 1)
                copy(merged_hi[:, ds(d, 1), :].rearrange("p k s -> p (k s)"), gate_a[:, :])\
                    .then_inc(merged_hi_done, 1)

            merge(0, FILL_C)
            for first_d, count, _, _ in TILES_C:
                with act.Fori(0, count) as i:
                    merge(i + first_d, i + (FILL_C + 4 + first_d))

            for n in range(NB):
                act.wait_ge(var_done, n + 1)
                nc.scalar.activation(norm[:, n, 1:2], norm[:, n, 0:1], ACT.Sqrt).then_inc(root_done, 1)
                act.wait_ge(scaled_by, n + 1)
                for c in [slice(0, D_MODEL)] if n < NB - 1 else halves:
                    nc.scalar.activation(rows[:, n, c], rows[:, n, c], ACT.Identity, scale=norm[:, n, 2:3],
                                         bias=norm[:, n, 3:4]).then_inc(normed, 1)

        @block.vector
        def _(dve):
            for s, credit in ((freed[0], 1), (roped_split, 1), (probs_ready, 1), (attn_split, 2),
                              (silu_done, 1), (scores_masked, 1), (pt_split, 1), (attn_gated, 2),
                              (convolved, 1), (conv_used, 1), (rnn_split, 1), (attn_in_used, 1),
                              (merged_split, 1)):
                dve.sem_inc(s, credit)

            def tt(dst, a, b, op):
                return nc.vector.tensor_tensor(dst, a, b, op)

            def stt(dst, a, scalar, b, op0, op1):
                return nc.vector.scalar_tensor_tensor(dst, a, scalar, b, op0, op1)

            steps = [0]

            def link(ins):
                steps[0] += 1
                ins.then_inc(dve_chain, 1)
                dve.wait_ge(dve_chain, steps[0])

            nc.vector.memset(v_lo[:, 0:HALF].bitcast(f32), 0.0).then_inc(v_zero, 1)
            for k in range(KT):
                dve.wait_ge(x_hi_done, k + 1)
                tt(xt_lo[:, k, :], x_raw[:, k, :], xt_hi[:, k, :].bitcast(f32), ALU.subtract)\
                    .then_inc(x_split, 1)
            dve.wait_ge(small_landed, 32)
            link(nc.vector.tensor_scalar(nsink[:, :], nsink[:, :], -1.0, None, ALU.mult))
            dve.wait_ge(consts_act, 1)
            e, s, s2 = nrate[:, :], norm_scratch[:, 0, :], norm_scratch[:, 1, :]
            acc = norm_scratch[:, 2, :]
            link(nc.vector.tensor_scalar(s, e, 2.0, None, ALU.add))
            link(nc.vector.reciprocal(s, s))
            link(tt(s, s, e, ALU.mult))
            link(tt(s2, s, s, ALU.mult))
            link(nc.vector.tensor_scalar(acc, s2, 1.0 / 19, None, ALU.mult))
            for odd in range(17, 1, -2):
                link(stt(acc, acc, 1.0 / odd, s2, ALU.add, ALU.mult))
            link(stt(acc, acc, 1.0, s, ALU.add, ALU.mult))
            link(nc.vector.tensor_scalar(s, par[:, LAMBDA:LAMBDA + 2 * RNN_BLOCKS], -1.0, 0.0,
                                         ALU.mult, ALU.max))
            link(stt(s, acc, 2.0, s, ALU.mult, ALU.add))
            link(nc.vector.tensor_scalar(rate[:, :], s, LRU_C, None, ALU.mult))
            link(nc.vector.tensor_scalar(nrate[:, :], s, -LRU_C, None, ALU.mult))
            dve.wait_ge(table_landed, 32)

            def rope(part, fill, col, count):
                if part == 0:
                    dve.wait_ge(filled[0], fill + 1)
                    dve.wait_ge(roped_split, count)
                    stt(rot_a[:, :], buf[0][:, :], bias(col), cos, ALU.add, ALU.mult)
                elif part == 1:
                    stt(rot_b[0:64, :], buf[0][64:P, :], par[64:P, ds(B_IN + col, 1)], sin[64:P, :],
                        ALU.add, ALU.mult)
                    stt(rot_b[64:P, :], buf[0][0:64, :], par[0:64, ds(B_IN + col, 1)], sin[0:64, :],
                        ALU.add, ALU.mult).then_inc(freed[0], 1)
                else:
                    dve.wait_ge(freed[0], fill + 2)
                    tt(rot_a[:, :], rot_a[:, :], rot_b[:, :], ALU.add).then_inc(roped, 1)

            def rope_lo(dst, hi, count):
                dve.wait_ge(roped_hi, count)
                tt(dst[:, :], rot_a[:, :], hi[:, :].bitcast(f32), ALU.subtract).then_inc(roped_split, 1)

            def silu(g, h):
                dve.wait_ge(freed[1], h + (g * FILLS_GROUP + 3))
                stt(gate[:, :], tanh_g[:, :], 1.0, gate[:, :], ALU.add, ALU.mult).then_inc(silu_done, 1)

            def gate_half(g, h, half):
                c = slice(half * HALF, (half + 1) * HALF)
                dve.wait_ge(silu_done, h + (g * HEADS + 2))
                dve.wait_ge(attn_split, h * 2 + (g * 2 * HEADS + half + 1))
                dve.wait_ge(pv_done, h * NB + (g * HEADS * NB + NB + (NB // 2 + 1, NB)[half]))
                tt(gated[:, c], ot_ps[:, c], gate[:, c], ALU.mult).then_inc(attn_gated, 1)

            def attention_lo(g, h, half):
                at = ds(h * SEQ + half * HALF, HALF)
                dve.wait_ge(attn_hi_done, h * 2 + (g * 2 * HEADS + half + 1))
                tt(at_lo[:, at], gated[:, half * HALF:(half + 1) * HALF], at_hi[:, at].bitcast(f32),
                   ALU.subtract).then_inc(attn_split, 1)

            def place_sink(g, h):
                dve.wait_ge(exp_done, h * NB + (g * HEADS * NB + 1))
                for dst in (masked[:, 3 * P:3 * P + 1], nsink_now[:, :]):
                    nc.vector.tensor_copy(dst, nsink[:, ds(h + g * HEADS, 1)]).then_inc(sink_placed, 1)
                dve.wait_ge(sink_placed, h * 2 + (g * 2 * HEADS + 2))

            def mask_scores(m, n):
                nk = len(key_blocks(n))
                c0 = (3 - nk) * P
                m0 = 0 if n else P
                dve.wait_ge(exp_done, m + n + 1)
                dve.wait_ge(scores_done, m + n + 2)
                dve.sem_inc(dve_waited, 1)
                nc.vector.tensor_tensor_reduce(
                    out=masked[:, c0:3 * P], in0=s_ps[:, 0:nk * P], in1=mask[:, m0:m0 + nk * P],
                    scale=-SCALE, scalar=nsink_now[:, 0:1], op0=ALU.add, op1=ALU.min,
                    accum_out=neg_max[:, 0:1]).then_inc(scores_masked, 1)

            def normalize(m, n):
                c0 = (3 - len(key_blocks(n))) * P
                dve.wait_ge(exp_done, m + n + 2)
                dve.wait_ge(probs_ready, m + n + 1)
                nc.vector.reciprocal(rdenom[:, :], denom[:, :]).then_inc(rdenom_done, 1)
                dve.wait_ge(rdenom_done, m + n + 1)
                nc.vector.tensor_scalar(probs[:, n % 2, c0:3 * P], probs[:, n % 2, c0:3 * P],
                                        rdenom[:, 0:1], None, ALU.mult).then_inc(probs_ready, 1)

            def attention(g, h, next_lo, next_hi, more):
                first_conv = next_lo is None
                m = h * NB + g * HEADS * NB
                turn = (h + (g * FILLS_GROUP + 2), h * 2 + (g * (2 + 2 * HEADS) + 4),
                        h + (g * (HEADS + 1) + 3))
                if next_lo is k_lo:
                    turn = (turn[0], (g + 1) * (2 + 2 * HEADS), turn[2])
                for n in range(1, NB + 3):
                    if n < NB:
                        mask_scores(m, n)
                        normalize(m, n)
                    if n == NB and first_conv:
                        conv_tap(0, 1)
                    if n <= NB:
                        q = n - 1
                        dve.wait_ge(pt_hi_done, m + q + 1)
                        for i, count, slot in pt_segments(q):
                            at = slice(slot, slot + 2 * count - 1, 2)
                            last = tt(pt_lo[:, at, :],
                                      pt_ps[:, i * P:(i + count) * P].rearrange("p (n c) -> p n c", c=P),
                                      pt_hi[:, at, :].bitcast(f32), ALU.subtract)
                        last.then_inc(pt_split, 1)
                    if n == 2:
                        silu(g, h)
                    if NB - 2 <= n <= NB and not first_conv:
                        rope(n - NB + 2, *turn)
                    if n == 1 and first_conv:
                        zero_padding()
                    if n == NB and first_conv:
                        conv_tap(0, 2)
                    if n == NB + 1:
                        gate_half(g, h, 0)
                        if first_conv:
                            conv_tap(0, 3)
                        if next_lo is not None:
                            rope_lo(next_lo, next_hi, turn[2])
                        attention_lo(g, h, 0)
                    if n == NB + 2:
                        if more:
                            place_sink(g, h + 1)
                            mask_scores(m + NB, 0)
                        gate_half(g, h, 1)
                        if first_conv:
                            conv_low(0)
                        if more:
                            normalize(m + NB, 0)
                        attention_lo(g, h, 1)

            def zero_padding():
                dve.wait_ge(roped_split, N_GROUPS * (HEADS + 1) + 1)
                for at, end in ((0, CONV_LEFT), (CONV_LEFT + SEQ, CONV_W + SEQ)):
                    nc.vector.memset(padded[:, at:end], 0.0).then_inc(padding_zero, 1)

            def conv_tap(b, tap):
                if tap == 1:
                    dve.wait_ge(conv_begun, b + 1)
                else:
                    dve.wait_ge(tap_done, b * (CONV_W - 2) + tap - 1)
                stt(conv[:, :], padded[:, tap:tap + SEQ], par[:, ds(b + CONV_WEIGHT + tap * RNN_BLOCKS, 1)],
                    conv[:, :], ALU.mult, ALU.add).then_inc(tap_done if tap < CONV_W - 1 else convolved, 1)

            def conv_low(b):
                dve.wait_ge(conv_hi_done, b + 1)
                tt(conv_lo[:, :], conv[:, :], conv_hi[:, :].bitcast(f32), ALU.subtract)\
                    .then_inc(conv_split, 1)

            def silu_gate(b, fill):
                dve.wait_ge(sigm_g_done, b + 1)
                stt(silu_g[:, :], buf[1][:, :], bias(b * 2 + B_RNN + 1), silu_g[:, :], ALU.add, ALU.mult)\
                    .then_inc(freed[1], 1)

            def block_head(b, fill, pair_before, j_before):
                for tap in range(1, CONV_W):
                    conv_tap(b, tap)
                finish_block(b - 1, pair_before, j_before)
                conv_low(b)
                silu_gate(b, fill)

            for part in range(3):
                rope(part, 0, 0, 1)
            rope_lo(k_lo, k_hi, 1)
            for g in range(N_GROUPS):
                for part in range(3):
                    rope(part, 1 + g * FILLS_GROUP, g * (2 + 2 * HEADS) + 2, g * (HEADS + 1) + 2)
                rope_lo(q_lo, q_hi, g * (HEADS + 1) + 2)
                dve.wait_ge(v_hi_done, g + 1)
                tt(v_lo[:, :], ot_ps[:, :], v_hi[:, :].bitcast(f32), ALU.subtract).then_inc(v_split, 1)
                place_sink(g, 0)
                mask_scores(g * HEADS * NB, 0)
                normalize(g * HEADS * NB, 0)
                with dve.Fori(0, HEADS - 1) as h:
                    attention(g, h, q_lo, q_hi, True)
                attention(g, HEADS - 1, *((k_lo, k_hi) if g < N_GROUPS - 1 else (None, None)), False)

            def recurrence(b, add):
                add(0)
                for d in range(2):
                    dve.wait_ge(gate_freed[d], b * 2 + 3)
                    last = tt(state[d][:, :], state[d][:, :], conv[:, :], ALU.mult)
                last.then_inc(conv_used, 1)
                for n in range(1, 4):
                    add(n)
                for d in range(2):
                    dve.wait_ge(squared, b * 2 + d + 1)
                    stt(root[d][:, :], square[:, :], 1.0, root[d][:, :], ALU.add, ALU.mult)\
                        .then_inc(one_less, 1)
                dve.wait_ge(conv_used, b + 2)
                for d in range(2):
                    dve.wait_ge(rooted, b * 2 + d + 1)
                    tt(state[d][:, :], state[d][:, :], root[d][:, :], ALU.mult).then_inc(u_done, 1)
                for d, turn in ((0, 1), (1, -1)):
                    dve.wait_ge(u_done, b * 2 + d + 1)
                    last = nc.vector.tensor_tensor_scan(state[d][:, ::turn], decay[d][:, ::turn],
                                                        state[d][:, ::turn], 0.0, ALU.mult, ALU.add)
                last.then_inc(scanned, 1)
                dve.wait_ge(scanned, b * 2 + 1)
                tt(state[0][:, :], state[0][:, :], state[1][:, :], ALU.add).then_inc(scanned, 1)
                dve.wait_ge(scanned, b * 2 + 2)
                tt(state[0][:, :], state[0][:, :], silu_g[:, :], ALU.mult).then_inc(rnn_done, 1)

            def finish_block(b, pair, j):
                dve.wait_ge(rnn_hi_done, b + 1)
                tt(h_lo[pair][:, j, :], state[0][:, :], h_hi[pair][:, j, :].bitcast(f32), ALU.subtract)\
                    .then_inc(rnn_split, 1)

            def add_branch(d, fill):
                b = d % 2
                dve.wait_ge(filled[b], fill + 1)
                tt(racc[:, d, :], buf[b][:, :], racc[:, d, :], ALU.add).then_inc(freed[b], 1)

            def nothing(n):
                return None

            silu_gate(0, FILL_X0)
            dve.wait_ge(attn_split, 2 * N_HEADS + 2)
            recurrence(0, nothing)
            block_head(1, FILL_X1, 0, 0)
            recurrence(1, nothing)
            dve.wait_ge(racc_zero, 1)
            for b in range(2):
                dve.wait_ge(spilled[b], 16 * (1 + 4 * N_GROUPS))
            with dve.Fori(0, (PAIRS - 1) // 2) as pp:
                for i in range(2):
                    for j in range(2):
                        b = pp * 4 + 2 + 2 * i + j
                        f = pp * (2 * FILLS_PAIR) + FILL_P + i * FILLS_PAIR + 3 * j
                        block_head(b, f, 1 - i if j else i, 1 - j)
                        recurrence(b, lambda n: add_branch(4 * j + n, f + 1 + n // 2))
            finish_block(RNN_BLOCKS - 1, (PAIRS - 1) % 2, 1)
            for d in range(KT):
                add_branch(d, FILL_C + 1 + d // 2)

            def merge(d, fill):
                dve.wait_ge(attn_in_landed, d * 16 + 16)
                tt(attn_in[:, 0, :], attn_in[:, 0, :], attn_in[:, 1, :], ALU.add).then_inc(mixed, 1)
                dve.wait_ge(freed[1], fill + 2)
                tt(gate_r[:, :], gate_r[:, :], racc[:, ds(d, 1), :].rearrange("p k s -> p (k s)"),
                   ALU.mult)
                dve.wait_ge(mixed, d + 1)
                tt(gate_a[:, :], gate_a[:, :], attn_in[:, 0, :], ALU.mult).then_inc(attn_in_used, 1)
                dve.wait_ge(attn_in_used, d + 2)
                tt(gate_a[:, :], gate_a[:, :], gate_r[:, :], ALU.add).then_inc(merged_done, 1)
                dve.wait_ge(merged_hi_done, d + 1)
                tt(merged_lo[:, ds(d, 1), :].rearrange("p k s -> p (k s)"), gate_a[:, :],
                   merged_hi[:, ds(d, 1), :].rearrange("p k s -> p (k s)").bitcast(f32),
                   ALU.subtract).then_inc(merged_split, 1)

            merge(0, FILL_C)
            for first_d, count, _, _ in TILES_C:
                with dve.Fori(0, count) as i:
                    merge(i + first_d, i + (FILL_C + 4 + first_d))

            dve.wait_ge(rows_landed, 16 * NB)
            dve.wait_ge(ln_landed, 48)
            for n in range(NB):
                stt(rows[:, n, :], rows[:, n, :], ALPHA, bias_o[:, :], ALU.mult, ALU.add)\
                    .then_inc(resid, 1)

            def apply_gain(n):
                dve.wait_ge(normed, n + 1)
                tt(rows[:, n, :], rows[:, n, :], gain[:, :], ALU.mult).then_inc(gained, 1)

            for half, c in enumerate(halves):
                for n in range(NB):
                    if half and n:
                        apply_gain(n - 1)
                    dve.wait_ge(resid, n + 1)
                    dve.wait_ge(out_done, half * NB + n + 1)
                    tt(rows[:, n, c], row_bank[n], rows[:, n, c], ALU.add).then_inc(out_added, 1)
                    dve.wait_ge(out_added, half * NB + n + 1)
                    nc.vector.bn_stats(stats[:, n, half, :], rows[:, n, c]).then_inc(stats_done, 1)
                    if half:
                        dve.wait_ge(stats_done, NB + n + 1)
                        link(nc.vector.bn_aggr(moments[:, n, :],
                                               stats[:, n, :, :].rearrange("p a b -> p (a b)")))
                        nc.vector.tensor_scalar(norm[:, n, 0:1], moments[:, n, 1:2], LN_EPS, None, ALU.add)\
                            .then_inc(var_done, 1)
                        dve.wait_ge(root_done, n + 1)
                        link(nc.vector.reciprocal(norm[:, n, 2:3], norm[:, n, 1:2]))
                        stt(norm[:, n, 3:4], moments[:, n, 0:1], -1.0, norm[:, n, 2:3], ALU.mult, ALU.mult)\
                            .then_inc(scaled_by, 1)
            for i, c in enumerate(halves):
                dve.wait_ge(normed, NB + i)
                tt(rows[:, NB - 1, c], rows[:, NB - 1, c], gain[:, c], ALU.mult).then_inc(gained, 1)
                dve.wait_ge(gained, NB + i)
                tt(rows[:, NB - 1, c], rows[:, NB - 1, c], shift[:, c], ALU.add).then_inc(last_shifted, 1)


def _tables():
    half = HEAD_DIM // 2
    inv = (np.float32(ROPE_THETA) ** (-np.arange(half, dtype=np.float32) * np.float32(2.0 / HEAD_DIM)))
    ang = inv.astype(np.float32)[:, None] * np.arange(SEQ, dtype=np.float32)[None, :]
    cos, sin = np.cos(ang).astype(np.float32), np.sin(ang).astype(np.float32)
    q, k = np.arange(P)[:, None], np.arange(3 * P)[None, :] - P
    mask = np.where(np.abs(q - k) <= P, 0.0, MASKED).astype(np.float32)
    return np.concatenate([np.concatenate([cos, cos]), np.concatenate([sin, -sin]), mask,
                           np.eye(P, dtype=np.float32)], axis=1)


def _stream(w_in, lru_wa, lru_wx, w_attn, w_rnn, w_out):
    def cols(w, at, n=P):
        return w[:, at:at + n].reshape(-1, P, n).transpose(1, 0, 2).reshape(P, -1)

    q0, k0, v0, ga0 = 0, 1024, 1280, 1536
    x0, gr0, ma0, mr0 = 2560, 3840, 5120, 6144
    def two(a, b):
        return [cols(w_in, a), cols(w_in, b)]

    def attn_branch(g):
        mine = w_attn[g * HEADS * P:(g + 1) * HEADS * P]
        return [cols(mine, d * P) for d in range(KT)]

    def rnn_branch(p, part):
        mine = w_rnn[2 * p * P:2 * (p + 1) * P]
        return [cols(mine, d * P) for d in range(part * KT // 2, (part + 1) * KT // 2)]

    def rnn_gates(b):
        return [lru_wa[0, b], lru_wa[1, b], lru_wx[0, b], lru_wx[1, b]]

    out = two(k0, v0)
    for g in range(N_GROUPS):
        for h in range(g * HEADS, (g + 1) * HEADS):
            out += two(q0 + h * P, ga0 + h * P)
        if g < N_GROUPS - 1:
            out += two(k0 + (g + 1) * P, v0 + (g + 1) * P) + attn_branch(g)
    branch = attn_branch(N_GROUPS - 1)
    out += two(x0, gr0) + rnn_gates(0) + branch[:KT // 2]
    out += two(x0 + P, gr0 + P) + rnn_gates(1) + branch[KT // 2:]
    for p in range(1, PAIRS):
        for j in range(2):
            b = 2 * p + j
            out += two(x0 + b * P, gr0 + b * P) + rnn_gates(b) + rnn_branch(p - 1, j)
    out += two(ma0, mr0) + rnn_branch(PAIRS - 1, 0) + rnn_branch(PAIRS - 1, 1)
    w_out_units = [cols(w_out[2 * k * P:2 * (k + 1) * P], h * HALF, HALF)
                   for h in range(2) for k in range(KT // 2)]
    for first_d, count, _, before in TILES_C:
        for d in range(first_d, first_d + count):
            out += two(ma0 + d * P, mr0 + d * P)
        out += w_out_units[before:before + 2] if before < 4 else w_out_units[4:]
    return np.concatenate(out, axis=1)


def _small(b_in, conv_w, conv_b, ba, bx, lam):
    b = b_in.reshape(56, P)
    q0, k0, v0, ga0, x0, gr0, ma0, mr0 = 0, 8, 10, 12, 20, 30, 40, 48
    order = []
    for g in range(N_GROUPS):
        order += [k0 + g, v0 + g]
        for h in range(g * HEADS, (g + 1) * HEADS):
            order += [q0 + h, ga0 + h]
    for n in range(RNN_BLOCKS):
        order += [x0 + n, gr0 + n]
    for d in range(KT):
        order += [ma0 + d, mr0 + d]
    rows = [b[order], conv_w.reshape(-1, P), conv_b.reshape(-1, P), ba.reshape(-1, P),
            bx.reshape(-1, P), lam.reshape(-1, P)]
    return np.ascontiguousarray(np.concatenate(rows, axis=0).T)


def kernel(x, w_in, b_in, attn_sink, conv_w, conv_b, lru_wa, lru_ba, lru_wx, lru_bx, lru_lambda,
           w_branch_attn, w_branch_rnn, w_out, b_out, ln_gain, ln_bias):
    import concourse.bacc as bacc
    from concourse.bass_utils import run_bass_kernel_spmd as run

    arrays = {
        "x_t": np.ascontiguousarray(np.asarray(x)[0].T.reshape(KT, P, SEQ).transpose(1, 0, 2)),
        "x_rows": np.ascontiguousarray(np.asarray(x)[0]),
        "stream": _stream(*(np.asarray(a)[0] for a in (w_in, lru_wa, lru_wx, w_branch_attn,
                                                       w_branch_rnn, w_out))),
        "small": _small(*(np.asarray(a)[0] for a in (b_in, conv_w, conv_b, lru_ba, lru_bx, lru_lambda))),
        "tables": _tables(),
        "sink": np.ascontiguousarray(np.asarray(attn_sink)[0]),
        "b_out": np.ascontiguousarray(np.asarray(b_out)[0]),
        "ln_gain": np.ascontiguousarray(np.asarray(ln_gain)[0]),
        "ln_bias": np.ascontiguousarray(np.asarray(ln_bias)[0]),
    }
    nc = bacc.Bacc("TRN2", target_bir_lowering=False, num_devices=1)
    args = [nc.dram_tensor(name, a.shape, mybir.dt.from_np(a.dtype), kind="ExternalInput").ap()
            for name, a in arrays.items()]
    args.append(nc.dram_tensor("out", (SEQ, D_MODEL), mybir.dt.float32, kind="ExternalOutput").ap())
    encoder_layer(nc, *args)
    r = run(nc, [arrays], core_ids=[0])
    return r.results[0]["out"].reshape(1, SEQ, D_MODEL)
```
